# Optimizing a Trainium2 kernel written in Bass

```python
import jax, jax.numpy as jnp
from jax import lax
import numpy as np
import math
import jax
import jax.numpy as jnp

D_MODEL = 1024
BATCH = 1
SEQ = 512
DEPTH = 2

N_A = DEPTH // 2
N_B = DEPTH - N_A
HEAD_DIM = 64
MEM_LEN = 256
N_MEM_HEADS = 4
MEM_WIDTH = N_MEM_HEADS * HEAD_DIM
MIX_WIDTH = D_MODEL - MEM_WIDTH
CONV_CH = MIX_WIDTH
CONV_WIDTH = 31
N_FOX_HEADS = MIX_WIDTH // HEAD_DIM
D_FF = 2816
FFN_CONV_WIDTH = 3
BLOCK_Q = 128
RMS_EPS = 1e-6
LN_EPS = 1e-5


def rmsnorm(x, g):
    xf = x.astype(jnp.float32)
    y = xf * lax.rsqrt(jnp.mean(xf * xf, axis=-1, keepdims=True) + RMS_EPS)
    return (y * g.astype(jnp.float32)).astype(x.dtype)

def layernorm(x, g, b):
    xf = x.astype(jnp.float32)
    mu = jnp.mean(xf, axis=-1, keepdims=True)
    var = jnp.mean(jnp.square(xf - mu), axis=-1, keepdims=True)
    y = (xf - mu) * lax.rsqrt(var + LN_EPS)
    return (y * g.astype(jnp.float32) + b.astype(jnp.float32)).astype(x.dtype)

def causal_dwconv(x, w, b):
    width, ch = w.shape
    y = lax.conv_general_dilated(
        x, w[:, None, :].astype(x.dtype), window_strides=(1,),
        padding=((width - 1, 0),), dimension_numbers=("NWC", "WIO", "NWC"),
        feature_group_count=ch)
    return y + b

def conformer_conv(u, b_glu, w_dw, b_dw, ln_g, ln_b):
    u = u + b_glu
    a, gate = jnp.split(u, 2, axis=-1)
    v = a * jax.nn.sigmoid(gate)
    v = causal_dwconv(v, w_dw, b_dw)
    v = layernorm(v, ln_g, ln_b)
    return jax.nn.silu(v)

def memory_attention(q, mem_k, mem_v):
    b, s, _ = q.shape
    qh = q.reshape(b, s, N_MEM_HEADS, HEAD_DIM)
    kh = mem_k.reshape(b, -1, N_MEM_HEADS, HEAD_DIM)
    vh = mem_v.reshape(b, -1, N_MEM_HEADS, HEAD_DIM)
    logits = jnp.einsum("bshd,bmhd->bhsm", qh, kh).astype(jnp.float32) * (HEAD_DIM ** -0.5)
    p = jax.nn.softmax(logits, axis=-1).astype(vh.dtype)
    o = jnp.einsum("bhsm,bmhd->bshd", p, vh)
    return o.reshape(b, s, MEM_WIDTH)

def forgetting_attention(q, k, v, cum_logf):
    b, s, h, dh = q.shape
    scale = dh ** -0.5
    outs = []
    for i in range(s // BLOCK_Q):
        q0 = i * BLOCK_Q
        kend = q0 + BLOCK_Q
        qb = q[:, q0:kend]
        kb = k[:, :kend]
        vb = v[:, :kend]
        logits = jnp.einsum("bqhd,bkhd->bhqk", qb, kb).astype(jnp.float32) * scale
        logits = logits + cum_logf[:, :, q0:kend, None] - cum_logf[:, :, None, :kend]
        qpos = q0 + jnp.arange(BLOCK_Q)
        kpos = jnp.arange(kend)
        logits = jnp.where(kpos[None, :] <= qpos[:, None], logits, -jnp.inf)
        p = jax.nn.softmax(logits, axis=-1).astype(vb.dtype)
        outs.append(jnp.einsum("bhqk,bkhd->bqhd", p, vb))
    return jnp.concatenate(outs, axis=1)

def conv_ffn(h, w_up, w_dw, b_dw, w_down):
    u = h @ w_up
    u = causal_dwconv(u, w_dw, b_dw)
    gate, val = jnp.split(u, 2, axis=-1)
    return (jax.nn.silu(gate) * val) @ w_down

def first_inputs(seed: int = 0) -> dict:
    key = jax.random.key(seed)
    ks = jax.random.split(key, 24)
    f32 = jnp.float32
    nrm = lambda k, shape, scale: jax.random.normal(k, shape, f32) * scale
    gain = lambda k, shape: 1.0 + 0.05 * jax.random.normal(k, shape, f32)
    d = D_MODEL
    return {
        "x": jax.random.normal(ks[0], (BATCH, SEQ, d), f32),
        "mem": jax.random.normal(ks[1], (BATCH, MEM_LEN, d), f32),
        "g_mix": gain(ks[2], (DEPTH, d)),
        "w_in_a": nrm(ks[3], (N_A, d, 2 * CONV_CH + MEM_WIDTH), d ** -0.5),
        "b_glu": nrm(ks[4], (N_A, 2 * CONV_CH), 0.02),
        "w_dw_a": nrm(ks[5], (N_A, CONV_WIDTH, CONV_CH), CONV_WIDTH ** -0.5),
        "b_dw_a": nrm(ks[6], (N_A, CONV_CH), 0.02),
        "ln_g": gain(ks[7], (N_A, CONV_CH)),
        "ln_b": nrm(ks[8], (N_A, CONV_CH), 0.02),
        "g_kv": gain(ks[9], (d,)),
        "w_kvf": nrm(ks[10], (d, 2 * MIX_WIDTH + N_FOX_HEADS), d ** -0.5),
        "b_f": 2.0 + 0.5 * jax.random.normal(ks[11], (N_FOX_HEADS,), f32),
        "w_in_b": nrm(ks[12], (N_B, d, MIX_WIDTH + MEM_WIDTH), d ** -0.5),
        "g_mem": gain(ks[13], (d,)),
        "w_mem_kv": nrm(ks[14], (DEPTH, d, 2 * MEM_WIDTH), d ** -0.5),
        "w_out": nrm(ks[15], (DEPTH, d, d), d ** -0.5),
        "g_ffn": gain(ks[16], (DEPTH, d)),
        "w_up": nrm(ks[17], (DEPTH, d, 2 * D_FF), d ** -0.5),
        "w_dw_f": nrm(ks[18], (DEPTH, FFN_CONV_WIDTH, 2 * D_FF), FFN_CONV_WIDTH ** -0.5),
        "b_dw_f": nrm(ks[19], (DEPTH, 2 * D_FF), 0.02),
        "w_down": nrm(ks[20], (DEPTH, D_FF, d), D_FF ** -0.5),
        "g_final": gain(ks[21], (d,)),
    }

def first_block(x, mem, g_mix, w_in_a, b_glu, w_dw_a, b_dw_a, ln_g, ln_b, g_kv, w_kvf, b_f,
              w_in_b, g_mem, w_mem_kv, w_out, g_ffn, w_up, w_dw_f, b_dw_f, w_down, g_final):
    bsz, seq, _ = x.shape
    mem_n = rmsnorm(mem, g_mem)
    k_sh = v_sh = cum_logf = None
    for l in range(DEPTH):
        h = rmsnorm(x, g_mix[l])
        mem_k, mem_v = jnp.split(mem_n @ w_mem_kv[l], 2, axis=-1)
        if l < N_A:
            p = h @ w_in_a[l]
            u, q_mem = p[..., :2 * CONV_CH], p[..., 2 * CONV_CH:]
            mix = conformer_conv(u, b_glu[l], w_dw_a[l], b_dw_a[l], ln_g[l], ln_b[l])
        else:
            if l == N_A:
                hk = rmsnorm(x, g_kv)
                kvf = hk @ w_kvf
                k_sh = kvf[..., :MIX_WIDTH].reshape(bsz, seq, N_FOX_HEADS, HEAD_DIM)
                v_sh = kvf[..., MIX_WIDTH:2 * MIX_WIDTH].reshape(bsz, seq, N_FOX_HEADS, HEAD_DIM)
                f_logit = (kvf[..., 2 * MIX_WIDTH:] + b_f).astype(jnp.float32)
                cum_logf = jnp.cumsum(jax.nn.log_sigmoid(f_logit), axis=1).transpose(0, 2, 1)
            p = h @ w_in_b[l - N_A]
            q, q_mem = p[..., :MIX_WIDTH], p[..., MIX_WIDTH:]
            q = q.reshape(bsz, seq, N_FOX_HEADS, HEAD_DIM)
            mix = forgetting_attention(q, k_sh, v_sh, cum_logf).reshape(bsz, seq, MIX_WIDTH)
        mem_o = memory_attention(q_mem, mem_k, mem_v)
        x = x + jnp.concatenate([mix, mem_o], axis=-1) @ w_out[l]
        x = x + conv_ffn(rmsnorm(x, g_ffn[l]), w_up[l], w_dw_f[l], b_dw_f[l], w_down[l])
    return rmsnorm(x, g_final)


ROPE_THETA = 10000.0
N_SB_HEADS = D_MODEL // (2 * HEAD_DIM)
N_DSA_HEADS = D_MODEL // (2 * HEAD_DIM)
N_IDX_HEADS = 4
IDX_DIM = 64
DSA_TOPK_MAX = 256
N_DIFF_HEADS = D_MODEL // (2 * HEAD_DIM)
DIFF_DIM = HEAD_DIM
D_FF_2 = ((-(-8 * D_MODEL // 3)) + 255) // 256 * 256
SB_W = N_SB_HEADS * HEAD_DIM
DSA_W = N_DSA_HEADS * HEAD_DIM
EVEN_SPLITS = (SB_W, SB_W, SB_W, DSA_W, HEAD_DIM, HEAD_DIM, N_IDX_HEADS * IDX_DIM, IDX_DIM, N_IDX_HEADS)
EVEN_IN = sum(EVEN_SPLITS)
EVEN_OUT = SB_W + DSA_W
DIFF_W = N_DIFF_HEADS * 2 * DIFF_DIM
N_EVEN = (DEPTH + 1) // 2
N_ODD = DEPTH // 2
ALPHA = (2 * DEPTH) ** 0.25
BETA = (8 * DEPTH) ** -0.25


F32 = jnp.float32

def layer_norm(x, g, b):
    x32 = x.astype(F32)
    mu = jnp.mean(x32, axis=-1, keepdims=True)
    var = jnp.mean(jnp.square(x32 - mu), axis=-1, keepdims=True)
    return ((x32 - mu) * lax.rsqrt(var + LN_EPS) * g.astype(F32) + b.astype(F32)).astype(x.dtype)

def rms_norm(x, g):
    x32 = x.astype(F32)
    ms = jnp.mean(jnp.square(x32), axis=-1, keepdims=True)
    return (x32 * lax.rsqrt(ms + LN_EPS) * g.astype(F32)).astype(x.dtype)

def rope_tables(positions, dim):
    inv = ROPE_THETA ** (-jnp.arange(0, dim, 2, dtype=F32) / dim)
    ang = positions.astype(F32)[..., None] * inv
    return jnp.cos(ang)[:, :, None, :], jnp.sin(ang)[:, :, None, :]

def apply_rope(t, cos, sin):
    t32 = t.astype(F32)
    half = t.shape[-1] // 2
    t1, t2 = t32[..., :half], t32[..., half:]
    return jnp.concatenate([t1 * cos - t2 * sin, t2 * cos + t1 * sin], axis=-1).astype(t.dtype)

def to_blocks(t):
    b, s = t.shape[:2]
    return t.reshape((b, s // BLOCK_Q, BLOCK_Q) + t.shape[2:]).swapaxes(0, 1)

def from_blocks(o):
    nb, b, bq = o.shape[:3]
    return o.swapaxes(0, 1).reshape((b, nb * bq) + o.shape[3:])

def stick_breaking_attention(q, k, v):
    s_len, d = q.shape[1], q.shape[-1]
    scale = d ** -0.5
    key_pos = jnp.arange(s_len)

    def block(args):
        qb, start = args
        z = jnp.einsum('bqhd,bshd->bhqs', qb, k, preferred_element_type=F32) * scale
        qpos = start + jnp.arange(BLOCK_Q)
        past = key_pos[None, :] < qpos[:, None]
        log_keep = jnp.where(past, jax.nn.log_sigmoid(-z), 0.0)
        suffix = lax.cumsum(log_keep, axis=3, reverse=True) - log_keep
        w = jnp.where(past, jnp.exp(jax.nn.log_sigmoid(z) + suffix), 0.0)
        return jnp.einsum('bhqs,bshd->bqhd', w.astype(v.dtype), v)

    starts = jnp.arange(s_len // BLOCK_Q) * BLOCK_Q
    return from_blocks(lax.map(block, (to_blocks(q), starts)))

def dsa_attention(q, k, v, q_idx, k_idx, w_idx):
    s_len, d = q.shape[1], q.shape[-1]
    topk = min(DSA_TOPK_MAX, s_len // 4)
    key_pos = jnp.arange(s_len)
    gather = jax.vmap(lambda t, i: t[i])

    def block(args):
        qb, qib, wb, start = args
        qpos = start + jnp.arange(BLOCK_Q)
        causal = key_pos[None, :] <= qpos[:, None]
        logits = jnp.einsum('bqhe,bse->bhqs', qib, k_idx, preferred_element_type=F32) * IDX_DIM ** -0.5
        score = jnp.einsum('bhqs,bqh->bqs', jax.nn.relu(logits), wb.astype(F32))
        score = jnp.where(causal[None], score, -jnp.inf)
        _, sel = lax.top_k(score, topk)
        valid = sel <= qpos[None, :, None]
        kg = gather(k, sel)
        vg = gather(v, sel)
        s = jnp.einsum('bqhd,bqkd->bhqk', qb, kg, preferred_element_type=F32) * d ** -0.5
        s = jnp.where(valid[:, None], s, -jnp.inf)
        p = jax.nn.softmax(s, axis=-1)
        return jnp.einsum('bhqk,bqkd->bqhd', p.astype(vg.dtype), vg)

    starts = jnp.arange(s_len // BLOCK_Q) * BLOCK_Q
    return from_blocks(lax.map(block, (to_blocks(q), to_blocks(q_idx), to_blocks(w_idx), starts)))

def diff_attention(q, k, v, lam):
    s_len, d = q.shape[1], q.shape[-1]
    key_pos = jnp.arange(s_len)

    def block(args):
        qb, start = args
        qpos = start + jnp.arange(BLOCK_Q)
        causal = key_pos[None, :] <= qpos[:, None]
        s = jnp.einsum('bqhcd,bshcd->bhcqs', qb, k, preferred_element_type=F32) * d ** -0.5
        p = jax.nn.softmax(jnp.where(causal, s, -jnp.inf), axis=-1)
        a = p[:, :, 0] - lam * p[:, :, 1]
        return jnp.einsum('bhqs,bshe->bqhe', a.astype(v.dtype), v)

    starts = jnp.arange(s_len // BLOCK_Q) * BLOCK_Q
    return from_blocks(lax.map(block, (to_blocks(q), starts)))

def even_mixer(h, cos, sin, w_in, w_out):
    b, s, _ = h.shape
    idx, acc = [], 0
    for width in EVEN_SPLITS[:-1]:
        acc += width
        idx.append(acc)
    q_sb, k_sb, v_sb, q_dsa, k_dsa, v_dsa, q_ix, k_ix, w_ix = jnp.split(h @ w_in, idx, axis=-1)
    o_sb = stick_breaking_attention(q_sb.reshape(b, s, N_SB_HEADS, HEAD_DIM),
                                    k_sb.reshape(b, s, N_SB_HEADS, HEAD_DIM),
                                    v_sb.reshape(b, s, N_SB_HEADS, HEAD_DIM))
    o_dsa = dsa_attention(apply_rope(q_dsa.reshape(b, s, N_DSA_HEADS, HEAD_DIM), cos, sin),
                          apply_rope(k_dsa[:, :, None], cos, sin)[:, :, 0],
                          v_dsa,
                          apply_rope(q_ix.reshape(b, s, N_IDX_HEADS, IDX_DIM), cos, sin),
                          apply_rope(k_ix[:, :, None], cos, sin)[:, :, 0],
                          w_ix * N_IDX_HEADS ** -0.5)
    o = jnp.concatenate([o_sb.reshape(b, s, SB_W), o_dsa.reshape(b, s, DSA_W)], axis=-1)
    return o @ w_out

def odd_mixer(h, cos, sin, w_in, lam_q1, lam_k1, lam_q2, lam_k2, subln_g, w_out, lambda_init):
    b, s, _ = h.shape
    q, k, v = jnp.split(h @ w_in, 3, axis=-1)
    q = apply_rope(q.reshape(b, s, 2 * N_DIFF_HEADS, DIFF_DIM), cos, sin).reshape(b, s, N_DIFF_HEADS, 2, DIFF_DIM)
    k = apply_rope(k.reshape(b, s, 2 * N_DIFF_HEADS, DIFF_DIM), cos, sin).reshape(b, s, N_DIFF_HEADS, 2, DIFF_DIM)
    v = v.reshape(b, s, N_DIFF_HEADS, 2 * DIFF_DIM)
    lam = (jnp.exp(jnp.sum(lam_q1.astype(F32) * lam_k1.astype(F32)))
           - jnp.exp(jnp.sum(lam_q2.astype(F32) * lam_k2.astype(F32))) + lambda_init)
    o = diff_attention(q, k, v, lam)
    o = rms_norm(o, subln_g) * (1.0 - lambda_init)
    return o.reshape(b, s, DIFF_W) @ w_out

def swiglu(h, w_gate, w_up, w_down):
    return (jax.nn.silu(h @ w_gate) * (h @ w_up)) @ w_down

def second_inputs(seed: int = 0) -> dict:
    key = jax.random.key(seed)
    ks = jax.random.split(key, 24)

    def nrm(i, shape, scale):
        return jax.random.normal(ks[i], shape, F32) * scale

    return {
        'x': nrm(0, (BATCH, SEQ, D_MODEL), 1.0),
        'c': nrm(1, (BATCH, D_MODEL), 1.0),
        'positions': jnp.broadcast_to(jnp.arange(SEQ, dtype=jnp.int32), (BATCH, SEQ)),
        'w_mod': nrm(2, (DEPTH, D_MODEL, 6 * D_MODEL), 0.1 * D_MODEL ** -0.5),
        'b_mod': nrm(3, (DEPTH, 6 * D_MODEL), 0.01),
        'w_in_even': nrm(4, (N_EVEN, D_MODEL, EVEN_IN), D_MODEL ** -0.5),
        'w_out_even': nrm(5, (N_EVEN, EVEN_OUT, D_MODEL), BETA * EVEN_OUT ** -0.5),
        'w_in_odd': nrm(6, (N_ODD, D_MODEL, 3 * DIFF_W), D_MODEL ** -0.5),
        'lam_q1': nrm(7, (N_ODD, DIFF_DIM), 0.1),
        'lam_k1': nrm(8, (N_ODD, DIFF_DIM), 0.1),
        'lam_q2': nrm(9, (N_ODD, DIFF_DIM), 0.1),
        'lam_k2': nrm(10, (N_ODD, DIFF_DIM), 0.1),
        'subln_g': 1.0 + nrm(11, (N_ODD, 2 * DIFF_DIM), 0.02),
        'w_out_odd': nrm(12, (N_ODD, DIFF_W, D_MODEL), BETA * DIFF_W ** -0.5),
        'ln_mix_g': 1.0 + nrm(13, (DEPTH, D_MODEL), 0.02),
        'ln_mix_b': nrm(14, (DEPTH, D_MODEL), 0.02),
        'w_gate': nrm(15, (DEPTH, D_MODEL, D_FF_2), D_MODEL ** -0.5),
        'w_up': nrm(16, (DEPTH, D_MODEL, D_FF_2), D_MODEL ** -0.5),
        'w_down': nrm(17, (DEPTH, D_FF_2, D_MODEL), BETA * D_FF_2 ** -0.5),
        'ln_ffn_g': 1.0 + nrm(18, (DEPTH, D_MODEL), 0.02),
        'ln_ffn_b': nrm(19, (DEPTH, D_MODEL), 0.02),
    }

def second_block(x, c, positions, w_mod, b_mod, w_in_even, w_out_even, w_in_odd, lam_q1, lam_k1,
              lam_q2, lam_k2, subln_g, w_out_odd, ln_mix_g, ln_mix_b, w_gate, w_up, w_down,
              ln_ffn_g, ln_ffn_b):
    cos, sin = rope_tables(positions, HEAD_DIM)
    mod = jnp.einsum('bd,ldm->lbm', jax.nn.silu(c), w_mod) + b_mod[:, None, :]
    for i in range(DEPTH):
        sh_m, sc_m, g_m, sh_f, sc_f, g_f = [t[:, None, :] for t in jnp.split(mod[i], 6, axis=-1)]
        h = x * (1.0 + sc_m) + sh_m
        if i % 2 == 0:
            y = even_mixer(h, cos, sin, w_in_even[i // 2], w_out_even[i // 2])
        else:
            j = i // 2
            lambda_init = 0.8 - 0.6 * math.exp(-0.3 * i)
            y = odd_mixer(h, cos, sin, w_in_odd[j], lam_q1[j], lam_k1[j], lam_q2[j], lam_k2[j],
                          subln_g[j], w_out_odd[j], lambda_init)
        x = layer_norm(ALPHA * x + (1.0 + g_m) * y, ln_mix_g[i], ln_mix_b[i])
        h = x * (1.0 + sc_f) + sh_f
        y = swiglu(h, w_gate[i], w_up[i], w_down[i])
        x = layer_norm(ALPHA * x + (1.0 + g_f) * y, ln_ffn_g[i], ln_ffn_b[i])
    return x


def setup_inputs(seed=0):
    out = dict(first_inputs(seed))
    for name, value in second_inputs(seed + 1).items():
        if name != "x":
            out[name + "_2"] = value
    return out


def reference(
    x, mem, g_mix, w_in_a, b_glu, w_dw_a, b_dw_a, ln_g, ln_b, g_kv, w_kvf, b_f, w_in_b, g_mem,
    w_mem_kv, w_out, g_ffn, w_up, w_dw_f, b_dw_f, w_down, g_final, c_2, positions_2, w_mod_2,
    b_mod_2, w_in_even_2, w_out_even_2, w_in_odd_2, lam_q1_2, lam_k1_2, lam_q2_2, lam_k2_2,
    subln_g_2, w_out_odd_2, ln_mix_g_2, ln_mix_b_2, w_gate_2, w_up_2, w_down_2, ln_ffn_g_2,
    ln_ffn_b_2,
):
    x = first_block(
        x, mem, g_mix, w_in_a, b_glu, w_dw_a, b_dw_a, ln_g, ln_b, g_kv, w_kvf, b_f, w_in_b,
        g_mem, w_mem_kv, w_out, g_ffn, w_up, w_dw_f, b_dw_f, w_down, g_final,
    )
    return second_block(
        x, c_2, positions_2, w_mod_2, b_mod_2, w_in_even_2, w_out_even_2, w_in_odd_2, lam_q1_2,
        lam_k1_2, lam_q2_2, lam_k2_2, subln_g_2, w_out_odd_2, ln_mix_g_2, ln_mix_b_2, w_gate_2,
        w_up_2, w_down_2, ln_ffn_g_2, ln_ffn_b_2,
    )


_drawn_inputs = setup_inputs


def setup_inputs(seed=0):
    import zlib

    import numpy as np

    out = dict(_drawn_inputs(seed))
    spreads = {}
    factors = {'b_glu': 3.468,
     'ln_b': 3.742,
     'g_kv': 2.741,
     'g_mem': 8.0,
     'b_mod_2': 4.014,
     'lam_q1_2': 6.522,
     'lam_k1_2': 5.073,
     'lam_q2_2': 4.9,
     'lam_k2_2': 8.0,
     'subln_g_2': 22.841,
     'b_dw_f': 3.641}
    for name, (base, spread) in spreads.items():
        noise = np.random.default_rng([zlib.crc32(name.encode()), seed]).standard_normal(out[name].shape)
        drawn = base * np.exp(spread * noise) if base else spread * noise
        out[name] = jnp.asarray(drawn.astype(out[name].dtype))
    for name, factor in factors.items():
        out[name] = (out[name] * factor).astype(out[name].dtype)
    return out
```

```python
import math
from contextlib import ExitStack

import concourse.bass as bass
from concourse import mybir

F32 = mybir.dt.float32
F32R = mybir.dt.float32r
I32 = mybir.dt.int32
ACT = mybir.ActivationFunctionType
ALU = mybir.AluOpType
AX = mybir.AxisListType

P = 128
D = 1024
KD = D // P
SEQ = 512
QT = SEQ // P
MEM = 256
DH = 64
CONV = 768
NCONV = CONV // P
TAPS = 31
FOX = CONV // DH
FF = 2816
FT = FF // P
HALF = FT // 2
TOPK = 128
IDX = 4
RMS_EPS = 1e-6
LN_EPS = 1e-5
ALPHA = 4.0 ** 0.25
LAMBDA_INIT = 0.8 - 0.6 * math.exp(-0.3)
SCALE = DH ** -0.5
MASKED = -(2.0 ** 100)
TAKEN = -3.4e38
LOWEST = -3.0e38
STRIP = 256
SLOT = HALF * STRIP
MOD_SLOTS = 4
MOD_STRIP = 3 * SEQ
GROUP = 32
TWO_PI_HIGH = 6.28125
TWO_PI_LOW = 2.0 * math.pi - TWO_PI_HIGH
ROUND = 1.5 * 2.0 ** 23
START = 16


def build(nc, a, out):
    ctx = ExitStack()
    with ctx:
        def sb(name, shape, dt=F32, where=ctx):
            return where.enter_context(nc.sbuf_tensor(name, shape, dt))

        xT = sb("xT", [P, KD, SEQ])
        raw = sb("raw", [P, 2, SLOT])
        wH = sb("wH", [P, 2, SLOT], F32R)
        wL = sb("wL", [P, 2, SLOT], F32R)
        ident = sb("ident", [P, P])
        identR = sb("identR", [P, P], F32R)
        ones = sb("ones", [P, P])
        causal = sb("causal", [P, P])
        causalR = sb("causalR", [P, P], F32R)
        before = sb("before", [P, P])
        beforeR = sb("beforeR", [P, P], F32R)
        neg_tri = sb("neg_tri", [P, P])
        neg_ones = sb("neg_ones", [P, P])
        memK = sb("memK", [P, 4, MEM])
        memV = sb("memV", [P, 4, MEM])
        cosT = sb("cosT", [P, SEQ])
        sinT = sb("sinT", [P, SEQ])
        mean = sb("mean", [P, SEQ])
        rstd = sb("rstd", [P, SEQ])
        tmpA = sb("tmpA", [P, 4, SEQ])
        tmpB = sb("tmpB", [P, 4, SEQ])
        small = sb("small", [P, 128])
        eps_rms, eps_ln = small[:, 0:1], small[:, 1:2]
        neg_lam, gate_bias = small[:, 2:3], small[:, 3:4]
        rope_const = small[:, 4:6]
        rope_inv, rope_sign = small[:, 4:5], small[:, 5:6]
        dots, dot_exp = small[:, 6:8], small[:, 8:10]
        neg_max, row_sum, row_inv = small[:, 16:32], small[:, 32:48], small[:, 48:64]
        head_sq, head_std = small[:, 64:96], small[:, 96:128]
        top8 = sb("top8", [P, 3, 8])
        lams = sb("lams", [P, 4, DH])
        mod = sb("mod", [P, 96])
        mod_plus = sb("mod_plus", [P, 96])
        silu_c = sb("silu_c", [P, KD, GROUP])

        def by_rows(v):
            return v.rearrange("l (n p) -> (l n) p", p=P)
        vectors = [
            ("g_mix", by_rows(a["g_mix"])), ("b_glu", by_rows(a["b_glu"])), ("b_dw_a", by_rows(a["b_dw_a"])),
            ("ln_g", by_rows(a["ln_g"])), ("ln_b", by_rows(a["ln_b"])),
            ("g_kv", a["g_kv"].rearrange("(n p) -> n p", p=P)), ("g_mem", a["g_mem"].rearrange("(n p) -> n p", p=P)),
            ("g_ffn", by_rows(a["g_ffn"])), ("g_final", a["g_final"].rearrange("(n p) -> n p", p=P)),
            ("c", by_rows(a["c_2"])), ("subln", a["subln_g_2"]),
            ("ln_mix_g", by_rows(a["ln_mix_g_2"])), ("ln_mix_b", by_rows(a["ln_mix_b_2"])),
            ("ln_ffn_g", by_rows(a["ln_ffn_g_2"])), ("ln_ffn_b", by_rows(a["ln_ffn_b_2"])),
            ("b_mod", by_rows(a["b_mod_2"])), ("b_dw_f", by_rows(a["b_dw_f"])),
            ("w_dw_a", a["w_dw_a"].rearrange("l t (n p) -> (l t n) p", p=P)),
            ("w_dw_f", a["w_dw_f"].rearrange("l t (n p) -> (l t n) p", p=P)),
        ]
        row_of, rows = {}, 0
        for name, v in vectors:
            row_of[name] = rows
            rows += v.shape[0]
        VT = -(-rows // P)
        cols = sb("cols", [P, VT * P])

        with ExitStack() as side:
            hH = sb("hH", [P, KD, SEQ], F32R, side)
            hL = sb("hL", [P, KD, SEQ], F32R, side)
        with ExitStack() as side:
            qS = sb("qS", [P, 2, SEQ], F32, side)
            kS = sb("kS", [P, 2, SEQ], F32, side)
            with ExitStack() as early:
                mod_ring = sb("mod_ring", [P, MOD_SLOTS, MOD_STRIP], F32, early)
            gate_rows = sb("gate_rows", [P, FOX, SEQ], F32, side)
        with ExitStack() as side:
            stickQ = sb("stickQ", [P, SEQ], F32, side)
            stickK = sb("stickK", [P, SEQ], F32, side)
            keep = sb("keep", [P, 2, 1280], F32, side)
            stick_w = sb("stick_w", [P, 2, 1280], F32, side)
        sb("side", [P, 2 * KD * SEQ])
        with ExitStack() as main:
            tok_x = sb("tok_x", [P, QT, D], F32, main)
            tok_mem = sb("tok_mem", [P, 2, D], F32, main)
            memT = sb("memT", [P, KD, MEM], F32, main)
            vec_rows = sb("vec_rows", [P, VT, P], F32, main)
            pos_int = sb("pos_int", [P, SEQ], I32, main)
            angle = sb("angle", [P, 4, SEQ], F32, main)
        with ExitStack() as main:
            gH = sb("gH", [P, HALF, SEQ], F32R, main)
            gL = sb("gL", [P, HALF, SEQ], F32R, main)
            ff_tmp = sb("ff_tmp", [P, 2, SEQ], F32, main)
        with ExitStack() as main:
            v_pad = sb("v_pad", [P, NCONV, SEQ + TAPS - 1], F32, main)
            y = sb("y", [P, NCONV, SEQ], F32, main)
            q_mem0 = sb("q_mem0", [P, 2, SEQ], F32, main)
            mod_rows = sb("mod_rows", [P, 8, SEQ], F32, main)
        with ExitStack() as main:
            foxQ = sb("foxQ", [P, 6, SEQ], F32, main)
            foxK = sb("foxK", [P, 6, SEQ], F32, main)
            foxV = sb("foxV", [P, QT, CONV], F32, main)
            q_mem1 = sb("q_mem1", [P, 2, SEQ], F32, main)
            with ExitStack() as before_heads:
                gate = sb("gate", [P, SEQ], F32, before_heads)
                pick = sb("pick", [P, FOX, P], F32, before_heads)
            gateS = sb("gateS", [P, 4, SEQ], F32, main)
        with ExitStack() as main:
            stQ = sb("stQ", [P, 4, SEQ], F32, main)
            stK = sb("stK", [P, 4, SEQ], F32, main)
            stV = sb("stV", [P, QT, 512], F32, main)
            spQ = sb("spQ", [P, 4, SEQ], F32, main)
            spK = sb("spK", [P, 2, SEQ], F32, main)
            ixQ = sb("ixQ", [P, 2, SEQ], F32, main)
            spV = sb("spV", [P, QT, 68], F32, main)
            chosen = sb("chosen", [P, QT, SEQ], F32, main)
        with ExitStack() as main:
            difQ = sb("difQ", [P, 8, SEQ], F32, main)
            difK = sb("difK", [P, 8, SEQ], F32, main)
            difV = sb("difV", [P, QT, D], F32, main)
        with ExitStack() as main:
            tok_out = sb("tok_out", [P, QT, D], F32, main)
        ps = ctx.enter_context(nc.psum_tensor("ps", [P, 8, SEQ], F32))

        def col(name, k):
            k = k + row_of[name]
            return cols[:, k:k + 1] if isinstance(k, int) else cols[:, bass.ds(k, 1)]

        def one_col(t, k):
            return t[:, k:k + 1] if isinstance(k, int) else t[:, bass.ds(k, 1)]

        def at(t, k, lo=0, hi=SEQ):
            return t[:, k, lo:hi] if isinstance(k, int) else t[:, bass.ds(k, 1), lo:hi].rearrange("p a n -> p (a n)")

        def span(t, lo, n):
            return t[:, :, lo:lo + n] if isinstance(lo, int) else t[:, :, bass.ds(lo, n)]

        class Signal:
            made = []

            def __init__(self, name, engine):
                self.sem = ctx.enter_context(nc.semaphore(name))
                self.count = START
                self.engine = engine
                Signal.made.append(self)

            def reserve(self, n):
                first = self.count
                self.count += n
                return first

        def sem(name):
            return ctx.enter_context(nc.semaphore(name))
        tensor_done, scalar_done, vector_done = sem("tensor_done"), sem("scalar_done"), sem("vector_done")
        constants_in, vectors_in, tokens_in, tables_in = sem("constants_in"), sem("vectors_in"), sem("tokens_in"), sem("tables_in")
        raw_landed = [sem("raw_landed0"), sem("raw_landed1")]
        raw_free = [sem("raw_free0"), sem("raw_free1")]
        mod_landed = [sem("mod_landed%d" % u) for u in range(MOD_SLOTS)]
        mod_free = [sem("mod_free%d" % u) for u in range(MOD_SLOTS)]
        out_written = sem("out_written")
        turn = {}
        strip_split = Signal("strip_split", "pool")
        tile_done = Signal("tile_done", "pe")
        summed, sums_in, turned_heads = Signal("summed", "pe"), Signal("sums_in", "pe"), Signal("turned_heads", "pe")
        logits_in, turned_in, value_in = Signal("logits_in", "pe"), Signal("turned_in", "pe"), Signal("value_in", "pe")
        stick_z, stick_sum, stick_pv = Signal("stick_z", "pe"), Signal("stick_sum", "pe"), Signal("stick_pv", "pe")
        index_in = Signal("index_in", "pe")
        mod_formed, mod_taken = Signal("mod_formed", "pe"), Signal("mod_taken", "act")
        taken_act = Signal("taken_act", "act")
        squares, roots, highs = Signal("squares", "act"), Signal("roots", "act"), Signal("highs", "act")
        swapped, gates = Signal("swapped", "act"), Signal("gates", "act")
        ff_pre, ff_silu, ff_high = Signal("ff_pre", "act"), Signal("ff_silu", "act"), Signal("ff_high", "act")
        staged, exp_in, turned_act = Signal("staged", "act"), Signal("exp_in", "act"), Signal("turned_act", "act")
        stick_log, stick_wt, relus = Signal("stick_log", "act"), Signal("stick_wt", "act"), Signal("relus", "act")
        taken_dve = Signal("taken_dve", "dve")
        parts, lows, centred = Signal("parts", "dve"), Signal("lows", "dve"), Signal("centred", "dve")
        ff_conv, ff_prod, ff_low = Signal("ff_conv", "dve"), Signal("ff_prod", "dve"), Signal("ff_low", "dve")
        max_in, turned_dve, head_out = Signal("max_in", "dve"), Signal("turned_dve", "dve"), Signal("head_out", "dve")
        stick_keep, stick_out, scored = Signal("stick_keep", "dve"), Signal("stick_out", "dve"), Signal("scored", "dve")

        def start_signals(eng, name):
            for s in Signal.made:
                if s.engine == name:
                    eng.sem_inc(s.sem, START)

        def alone(eng, i):
            if not isinstance(i, int):
                eng.sem_inc(turn[id(eng)], 1)

        def turns(eng, n, first=0):
            if n - first > 1:
                with eng.Fori(first, n) as i:
                    yield i
            elif n - first == 1:
                yield first

        def strips(eng, n, first=0):
            for i in turns(eng, n // 2, first):
                yield i * 2, 0, i
                yield i * 2 + 1, 1, i
            if n % 2 and n // 2 >= first:
                yield n - 1, 0, n // 2

        class Run:
            raws = splits = 0
            landed = [0, 0]

            def __init__(self, form, count, kt, pieces, take, width=STRIP, npieces=2, tokens=SEQ):
                self.form, self.count, self.kt, self.pieces, self.take = form, count, kt, pieces, take
                self.width, self.npieces, self.tokens = width, npieces, tokens
                self.r0, self.n0 = Run.raws, Run.splits
                self.landed0 = [Run.landed[(self.r0 + u) % 2] for u in range(2)]
                Run.raws += count
                for s in range(count):
                    Run.landed[(self.r0 + s) % 2] += 16 * npieces
                Run.splits += count
                self.tile0 = tile_done.reserve(2 * count)
                self.split0 = strip_split.reserve(count)
                self.act0, self.dve0 = taken_act.count, taken_dve.count
                if take.by_act:
                    taken_act.reserve(count)
                if take.by_dve:
                    taken_dve.reserve(count)
                take.attach(self)
                runs.append(self)

            def raw_slot(self, u):
                return (self.r0 + u) % 2

            def part_slot(self, u):
                return (self.n0 + u) % 2

            def bank(self, u, f):
                return 2 * self.part_slot(u) + f

            def wait_landed(self, eng, u, i):
                size = 16 * self.npieces
                eng.wait_ge(raw_landed[self.raw_slot(u)], i * size + (self.landed0[u] + size))
                alone(eng, i)

            def load(self, sp):
                for s, u, i in strips(sp, self.count):
                    slot = self.raw_slot(u)
                    to = raw[:, slot, 0:self.kt * self.width].rearrange("p (k c) -> p k c", k=self.kt)
                    pieces = self.pieces(s)
                    sp.wait_ge(raw_free[slot], i + ((self.r0 + u) // 2 + 1))
                    alone(sp, i)
                    for lo, hi, src in pieces:
                        sp.dma_start(to[:, :, lo:hi], src).then_inc(raw_landed[slot], 16)

            def split(self, pool):
                n = self.kt * self.width
                for s, u, i in strips(pool, self.count):
                    slot, part = self.raw_slot(u), self.part_slot(u)
                    self.wait_landed(pool, u, i)
                    pool.wait_ge(tile_done.sem, s * 2 + (self.tile0 - 2))
                    alone(pool, s)
                    pool.tensor_tensor(wH[:, part, 0:n], raw[:, slot, 0:n], ones[:, 0:1].to_broadcast([P, n]), ALU.mult)
                    pool.drain()
                    pool.tensor_tensor(wL[:, part, 0:n], raw[:, slot, 0:n], wH[:, part, 0:n].bitcast(F32),
                                       ALU.subtract).then_inc(strip_split.sem, 1)
                    pool.drain().then_inc(raw_free[slot], 1)

            def multiply_strip(self, pe, s, u, srcH, srcL, gate=None):
                part, w = self.part_slot(u), self.width
                pe.wait_ge(strip_split.sem, s + (self.split0 + 1))
                alone(pe, s)
                pe.wait_ge(taken_act.sem, s + (self.act0 - 1) if self.take.by_act else self.act0)
                alone(pe, s)
                pe.wait_ge(taken_dve.sem, s + (self.dve0 - 1) if self.take.by_dve else self.dve0)
                alone(pe, s)
                products = [(wH, srcH, "high"), (wL, srcH, None), (wH, srcL, "low")]
                for f in range(2):
                    bank = self.bank(u, f)
                    groups = []
                    if self.form == "A" and f * P < w:
                        groups.append((ps[:, bank, 0:self.tokens], lambda wp, hp, k: (
                            wp[:, part, k * w + f * P:k * w + f * P + P], hp[:, k, 0:self.tokens])))
                    elif self.form == "B":
                        for j in range(2):
                            t = (2 * f + j) * P
                            if t < self.tokens:
                                groups.append((ps[:, bank, j * w:j * w + w], lambda wp, hp, k, t=t: (
                                    hp[:, k, t:t + P], wp[:, part, k * w:k * w + w])))
                    for dst, operands in groups:
                        for t, (wp, hp, which) in enumerate(products):
                            for k in range(self.kt):
                                if gate and f == 0:
                                    gate(pe, which, k)
                                left, right = operands(wp, hp, k)
                                last = pe.matmul(dst, left, right, start=(t == 0 and k == 0), stop=(t == 2 and k == self.kt - 1))
                    if groups:
                        last.then_inc(tile_done.sem, 1)
                    else:
                        pe.drain().then_inc(tile_done.sem, 1)

            def multiply(self, pe, srcH, srcL, gate=None):
                if gate:
                    for u in range(min(2, self.count)):
                        self.multiply_strip(pe, u, u, srcH, srcL, gate if u == 0 else None)
                for s, u, i in strips(pe, self.count, 1 if gate else 0):
                    if not (gate and self.count == 1):
                        self.multiply_strip(pe, s, u, srcH, srcL)

            def wait_tile(self, eng, s, f):
                eng.wait_ge(tile_done.sem, s * 2 + (self.tile0 + f + 1))
                alone(eng, s)

        runs = []

        def columns(w, lo, n, k0=0, kt=KD):
            return span(w.rearrange("(k p) c -> p k c", p=P)[:, k0:k0 + kt, :], lo, n)

        def plain(w, lo=0, k0=0, kt=KD):
            return lambda s: [(0, P, columns(w, s * STRIP + lo, P, k0, kt)), (P, STRIP, columns(w, s * STRIP + (lo + P), P, k0, kt))]

        def pairs_of(w1, lo1, w2, lo2):
            return lambda s: [(0, P, columns(w1, s * P + lo1, P)), (P, STRIP, columns(w2, s * P + lo2, P))]

        class Take:
            by_act = by_dve = True

            def attach(self, run):
                self.run = run

            def scalar(self, act):
                pass

        class TakeCopy(Take):
            def __init__(self, dst, n=SEQ, first=0):
                self.dst, self.n, self.first = dst, n, first

            def scalar(self, act):
                r = self.run
                for s, u, i in strips(act, r.count):
                    r.wait_tile(act, s, 0)
                    act.activation(at(self.dst, s * 2 + self.first, 0, self.n), ps[:, r.bank(u, 0), 0:self.n],
                                   ACT.Copy).then_inc(taken_act.sem, 1)

            def vector(self, dve):
                r = self.run
                for s, u, i in strips(dve, r.count):
                    r.wait_tile(dve, s, 1)
                    dve.tensor_copy(at(self.dst, s * 2 + (self.first + 1), 0, self.n), ps[:, r.bank(u, 1), 0:self.n]
                                    ).then_inc(taken_dve.sem, 1)

        class TakeValues(Take):
            def __init__(self, dst):
                self.dst = dst

            def bank(self, u, f):
                r = self.run
                return ps[:, r.bank(u, f), 0:2 * r.width].rearrange("p (t c) -> p t c", t=2)

            def scalar(self, act):
                r = self.run
                for s, u, i in strips(act, r.count):
                    r.wait_tile(act, s, 0)
                    act.activation(span(self.dst[:, 0:2, :], s * r.width, r.width), self.bank(u, 0), ACT.Copy
                                   ).then_inc(taken_act.sem, 1)

            def vector(self, dve):
                r = self.run
                for s, u, i in strips(dve, r.count):
                    r.wait_tile(dve, s, 1)
                    dve.tensor_copy(span(self.dst[:, 2:4, :], s * r.width, r.width), self.bank(u, 1)
                                    ).then_inc(taken_dve.sem, 1)

        class TakeMemV(Take):
            def __init__(self, layer):
                self.layer = layer

            def scalar(self, act):
                self.run.wait_tile(act, 0, 0)
                act.activation(memV[:, 2 * self.layer, :], ps[:, self.run.bank(0, 0), 0:MEM], ACT.Copy).then_inc(taken_act.sem, 1)

            def vector(self, dve):
                self.run.wait_tile(dve, 0, 1)
                dve.wait_ge(taken_act.sem, self.run.act0 + 1)
                dve.tensor_copy(memV[:, 2 * self.layer + 1, :], ps[:, self.run.bank(0, 0), MEM:2 * MEM]).then_inc(taken_dve.sem, 1)

        class TakeRope(Take):
            by_act = False

            def __init__(self, dst):
                self.dst = dst

            def attach(self, run):
                self.run = run
                self.swap0 = swapped.reserve(2 * run.count)

            def scalar(self, act):
                r = self.run
                for s, u, i in strips(act, r.count):
                    act.wait_ge(taken_dve.sem, s + (r.dve0 - 1))
                    alone(act, s)
                    for f in range(2):
                        r.wait_tile(act, s, f)
                        for q in range(4):
                            o = 32 * (q ^ 1)
                            last = act.activation(tmpA[o:o + 32, r.bank(u, f), :], ps[32 * q:32 * q + 32, r.bank(u, f), :], ACT.Copy)
                        last.then_inc(swapped.sem, 1)

            def vector(self, dve):
                r = self.run
                for s, u, i in strips(dve, r.count):
                    for f in range(2):
                        dve.wait_ge(swapped.sem, s * 2 + (self.swap0 + f + 1))
                        alone(dve, s)
                        k = r.bank(u, f)
                        dve.tensor_tensor(tmpB[:, k, :], ps[:, r.bank(u, f), :], cosT[:, :], ALU.mult)
                        dve.tensor_tensor(tmpA[:, k, :], tmpA[:, k, :], sinT[:, :], ALU.mult)
                        dve.drain()
                        dve.tensor_tensor(at(self.dst, s * 2 + f), tmpB[:, k, :], tmpA[:, k, :], ALU.add)
                    dve.drain().then_inc(taken_dve.sem, 1)

        class TakeResidual(Take):
            by_act = False

            def __init__(self, gain=None):
                self.gain = gain

            def vector(self, dve):
                r = self.run
                for s, u, i in strips(dve, r.count):
                    for f in range(2):
                        r.wait_tile(dve, s, f)
                        t, x = ps[:, r.bank(u, f), :], at(xT, s * 2 + f)
                        if self.gain is None:
                            last = dve.tensor_tensor(x, t, x, ALU.add)
                        else:
                            last = dve.scalar_tensor_tensor(x, t, one_col(mod_plus, s * 2 + (self.gain + f)), x, ALU.mult, ALU.add)
                    last.then_inc(taken_dve.sem, 1)

        class TakeGlu(Take):
            by_act = False

            def attach(self, run):
                self.run = run
                self.gate0 = gates.reserve(run.count)

            def scalar(self, act):
                r = self.run
                for s, u, i in strips(act, r.count):
                    r.wait_tile(act, s, 1)
                    act.wait_ge(taken_dve.sem, s + (r.dve0 - 1))
                    alone(act, s)
                    act.activation(tmpA[:, u, :], ps[:, r.bank(u, 1), :], ACT.Sigmoid, bias=col("b_glu", s + NCONV)
                                   ).then_inc(gates.sem, 1)

            def vector(self, dve):
                r = self.run
                for s, u, i in strips(dve, r.count):
                    dve.wait_ge(gates.sem, s + (self.gate0 + 1))
                    alone(dve, s)
                    dve.scalar_tensor_tensor(at(v_pad, s, TAPS - 1, TAPS - 1 + SEQ), ps[:, r.bank(u, 0), :], col("b_glu", s),
                                             tmpA[:, u, :], ALU.add, ALU.mult).then_inc(taken_dve.sem, 1)

        class TakeForget(Take):
            by_dve = False

            def scalar(self, act):
                self.run.wait_tile(act, 0, 0)
                act.activation(gate[0:FOX, :], ps[0:FOX, self.run.bank(0, 0), :], ACT.Identity, bias=gate_bias[0:FOX, :]
                               ).then_inc(taken_act.sem, 1)

            def vector(self, dve):
                pass

        class TakeFF(Take):
            by_act = False

            def __init__(self, half, conv=None):
                self.half, self.conv = half, conv

            def attach(self, run):
                self.run = run
                n = run.count
                self.pre0 = ff_pre.reserve(n) if self.conv is not None else 0
                self.conv0 = ff_conv.reserve(n) if self.conv is not None else 0
                self.silu0, self.high0 = ff_silu.reserve(n), ff_high.reserve(n)
                self.prod0, self.low0 = ff_prod.reserve(n), ff_low.reserve(n)

            def weight(self, tap, s, f):
                k = tap * 2 * FT + f * FT + self.half * HALF
                return col("w_dw_f", s + (self.conv * 3 * 2 * FT + k))

            def scalar(self, act):
                r = self.run
                for s, u, i in strips(act, r.count):
                    if self.conv is not None:
                        act.wait_ge(ff_prod.sem, s + (self.prod0 - 1))
                        alone(act, s)
                        for f in range(2):
                            r.wait_tile(act, s, f)
                            bias = col("b_dw_f", s + (self.conv * 2 * FT + f * FT + self.half * HALF))
                            last = act.activation(tmpA[:, 2 * u + f, :], ps[:, r.bank(u, f), :], ACT.Identity, bias=bias,
                                                  scale=self.weight(2, s, f))
                        last.then_inc(ff_pre.sem, 1)
                        act.wait_ge(ff_conv.sem, s + (self.conv0 + 1))
                        alone(act, s)
                        gate_in = tmpA[:, 2 * u, :]
                    else:
                        act.wait_ge(ff_prod.sem, s + (self.prod0 - 1))
                        alone(act, s)
                        r.wait_tile(act, s, 0)
                        gate_in = ps[:, r.bank(u, 0), :]
                    act.activation(tmpB[:, u, :], gate_in, ACT.Silu).then_inc(ff_silu.sem, 1)
                    act.wait_ge(ff_prod.sem, s + (self.prod0 + 1))
                    alone(act, s)
                    act.activation(at(gH, s), ff_tmp[:, u, :], ACT.Copy).then_inc(ff_high.sem, 1)

            def vector(self, dve):
                r = self.run
                for s, u, i in strips(dve, r.count):
                    if self.conv is not None:
                        dve.wait_ge(ff_pre.sem, s + (self.pre0 + 1))
                        alone(dve, s)
                        for back in (1, 2):
                            for f in range(2):
                                t = tmpA[:, 2 * u + f, back:SEQ]
                                last = dve.scalar_tensor_tensor(t, ps[:, r.bank(u, f), 0:SEQ - back], self.weight(2 - back, s, f),
                                                                t, ALU.mult, ALU.add)
                            dve.drain()
                        dve.drain().then_inc(ff_conv.sem, 1)
                        value = tmpA[:, 2 * u + 1, :]
                    else:
                        r.wait_tile(dve, s, 1)
                        value = ps[:, r.bank(u, 1), :]
                    dve.wait_ge(ff_silu.sem, s + (self.silu0 + 1))
                    alone(dve, s)
                    dve.tensor_tensor(ff_tmp[:, u, :], value, tmpB[:, u, :], ALU.mult).then_inc(ff_prod.sem, 1)
                    dve.drain().then_inc(taken_dve.sem, 1)
                    dve.wait_ge(ff_high.sem, s + (self.high0 + 1))
                    alone(dve, s)
                    dve.tensor_tensor(at(gL, s), ff_tmp[:, u, :], at(gH, s).bitcast(F32), ALU.subtract).then_inc(ff_low.sem, 1)

            def gate(self, pe, which, k):
                if which == "high":
                    pe.wait_ge(ff_high.sem, self.high0 + k + 1)
                elif which == "low":
                    pe.wait_ge(ff_low.sem, self.low0 + k + 1)

        class Parts:
            tiles = range(KD)

            def reserve(self):
                self.high0, self.low0 = highs.reserve(len(self.tiles)), lows.reserve(len(self.tiles))

            def gate(self, pe, which, k):
                if k in self.tiles:
                    n = k - self.tiles[0] + 1
                    if which == "high":
                        pe.wait_ge(highs.sem, self.high0 + n)
                    elif which == "low":
                        pe.wait_ge(lows.sem, self.low0 + n)

            def tensor(self, pe):
                pass

            def scalar(self, act):
                for k in range(KD):
                    act.wait_ge(parts.sem, self.part0 + k + 1)
                    act.activation(hH[:, k, 0:self.n], tmpB[:, k % 4, 0:self.n], ACT.Copy).then_inc(highs.sem, 1)

            def low(self, dve, k):
                dve.wait_ge(highs.sem, self.high0 + k + 1)
                dve.tensor_tensor(hL[:, k, 0:self.n], tmpB[:, k % 4, 0:self.n], hH[:, k, 0:self.n].bitcast(F32),
                                  ALU.subtract).then_inc(lows.sem, 1)

        def square_sum(pe, square0, bank, tiles, n):
            for k in range(tiles):
                pe.wait_ge(squares.sem, square0 + k + 1)
                pe.matmul(ps[:, bank, 0:n], ones[:, :], tmpA[:, k % 4, 0:n], start=(k == 0), stop=(k == tiles - 1)
                          ).then_inc(summed.sem, 1)

        def square_tiles(act, src, square0, summed0, tiles, n, centred0=None):
            for k in range(tiles):
                if centred0 is not None:
                    act.wait_ge(centred.sem, centred0 + k + 1)
                act.wait_ge(summed.sem, summed0 + k - 3)
                act.activation(tmpA[:, k % 4, 0:n], src[:, k, 0:n], ACT.Square).then_inc(squares.sem, 1)

        class RmsParts(Parts):
            def __init__(self, src, name, g0=0, n=SEQ, again=False):
                self.src, self.name, self.g0, self.n, self.again = src, name, g0, n, again
                if not again:
                    self.square0, self.summed0, self.root0 = squares.reserve(KD), summed.reserve(KD), roots.reserve(1)
                self.part0 = parts.reserve(KD)
                self.reserve()

            def tensor(self, pe):
                if not self.again:
                    square_sum(pe, self.square0, 7, KD, self.n)

            def scalar(self, act):
                if not self.again:
                    square_tiles(act, self.src, self.square0, self.summed0, KD, self.n)
                    act.wait_ge(summed.sem, self.summed0 + KD)
                    act.activation(mean[:, 0:self.n], ps[:, 7, 0:self.n], ACT.Sqrt, bias=eps_rms, scale=1.0 / D).then_inc(roots.sem, 1)
                Parts.scalar(self, act)

            def vector(self, dve):
                if not self.again:
                    dve.wait_ge(roots.sem, self.root0 + 1)
                    dve.reciprocal(rstd[:, 0:self.n], mean[:, 0:self.n])
                    dve.drain()
                for k in range(KD):
                    dve.scalar_tensor_tensor(tmpB[:, k % 4, 0:self.n], self.src[:, k, 0:self.n], col(self.name, self.g0 + k),
                                             rstd[:, 0:self.n], ALU.mult, ALU.mult).then_inc(parts.sem, 1)
                    if k:
                        self.low(dve, k - 1)
                self.low(dve, KD - 1)

        class ModParts(Parts):
            n = SEQ

            def __init__(self, layer, shift, scale):
                self.shift, self.scale = 48 * layer + KD * shift, 48 * layer + KD * scale
                self.part0 = parts.reserve(KD)
                self.reserve()

            def scalar(self, act):
                for k in range(KD):
                    act.wait_ge(parts.sem, self.part0 + k + 1)
                    act.activation(hH[:, k, :], tmpB[:, k % 4, :], ACT.Copy).then_inc(highs.sem, 1)
                    act.activation(xT[:, k, :], xT[:, k, :], ACT.Copy, scale=ALPHA)

            def vector(self, dve):
                for k in range(KD):
                    dve.tensor_scalar(tmpB[:, k % 4, :], xT[:, k, :], mod_plus[:, self.scale + k:self.scale + k + 1],
                                      mod[:, self.shift + k:self.shift + k + 1], ALU.mult, ALU.add).then_inc(parts.sem, 1)
                    if k:
                        self.low(dve, k - 1)
                self.low(dve, KD - 1)

        class HeadParts(Parts):
            def __init__(self, sources, first=0, gain=None, factor=1.0):
                self.sources, self.gain, self.factor = sources, gain, factor
                self.tiles = range(first, first + len(sources))
                self.turn0 = turned_heads.reserve(len(sources))
                self.reserve()

            def tensor(self, pe):
                for n, (src, t) in enumerate(self.sources):
                    pe.wait_ge(lows.sem, self.low0 + n - 3)
                    for q in range(QT):
                        pe.transpose(ps[:, 4 + n % 4, q * P:q * P + P], src[:, t, q * P:q * P + P], ident[:, :])
                    pe.drain().then_inc(turned_heads.sem, 1)

            def scalar(self, act):
                for n, k in enumerate(self.tiles):
                    act.wait_ge(turned_heads.sem, self.turn0 + n + 1)
                    act.activation(hH[:, k, :], ps[:, 4 + n % 4, :], ACT.Copy,
                                   scale=1.0 if self.gain is None else self.gain).then_inc(highs.sem, 1)

            def vector(self, dve):
                for n, k in enumerate(self.tiles):
                    dve.wait_ge(highs.sem, self.high0 + n + 1)
                    dve.scalar_tensor_tensor(hL[:, k, :], ps[:, 4 + n % 4, :], 1.0 if self.gain is None else self.gain,
                                             hH[:, k, :].bitcast(F32), ALU.mult, ALU.subtract).then_inc(lows.sem, 1)

        stages = []

        class Stage:
            def __init__(self):
                stages.append(self)

            def tensor(self, pe):
                pass

            def scalar(self, act):
                pass

            def vector(self, dve):
                pass

        class Products(Stage):
            def __init__(self, prepare, *made):
                super().__init__()
                self.prepare, self.runs = prepare, made

            def tensor(self, pe):
                self.prepare.tensor(pe)
                for n, run in enumerate(self.runs):
                    run.multiply(pe, hH, hL, self.prepare.gate if n == 0 else None)

            def scalar(self, act):
                self.prepare.scalar(act)
                for run in self.runs:
                    run.take.scalar(act)

            def vector(self, dve):
                self.prepare.vector(dve)
                for run in self.runs:
                    run.take.vector(dve)

        class FeedForward(Stage):
            def __init__(self, prepare, up, down, gain=None, conv=None):
                super().__init__()
                self.prepare = prepare
                self.halves = []
                for h in range(2):
                    go_up = Run("A", HALF, KD, up(h), TakeFF(h, conv))
                    go_down = Run("A", D // STRIP, HALF, plain(down, 0, h * HALF, HALF), TakeResidual(gain))
                    self.halves.append((go_up, go_down))

            def tensor(self, pe):
                self.prepare.tensor(pe)
                for h, (up, down) in enumerate(self.halves):
                    up.multiply(pe, hH, hL, self.prepare.gate if h == 0 else None)
                    down.multiply(pe, gH, gL, up.take.gate)

            def scalar(self, act):
                self.prepare.scalar(act)
                for up, down in self.halves:
                    up.take.scalar(act)

            def vector(self, dve):
                self.prepare.vector(dve)
                for up, down in self.halves:
                    up.take.vector(dve)
                    down.take.vector(dve)

        class Constants(Stage):
            def tensor(self, pe):
                pe.wait_ge(constants_in, 1)
                pe.wait_ge(vectors_in, 16 * len(vector_loads))
                for j in range(VT):
                    pe.transpose(ps[:, j // 4, (j % 4) * P:(j % 4) * P + P], vec_rows[:, j, :], ident[:, :])

            def vector(self, dve):
                dve.wait_ge(constants_in, 1)
                dve.tensor_copy(identR[:, :], ident[:, :])
                dve.tensor_copy(causalR[:, :], causal[:, :])
                dve.tensor_copy(beforeR[:, :], before[:, :])
                dve.memset(eps_rms, RMS_EPS)
                dve.memset(eps_ln, LN_EPS)

        class Tables(Stage):
            def tensor(self, pe):
                pe.wait_ge(tokens_in, 32)
                n = 0
                for src, tiles in ((tok_mem, 2), (tok_x, QT)):
                    for k in range(KD):
                        pe.wait_ge(highs.sem, self.high0 + n - 3)
                        for t in range(tiles):
                            pe.transpose(ps[:, 4 + n % 4, t * P:t * P + P], src[:, t, k * P:k * P + P], ident[:, :])
                        pe.drain().then_inc(turned_heads.sem, 1)
                        n += 1

            def __init__(self):
                super().__init__()
                self.turn0, self.high0 = turned_heads.reserve(2 * KD), highs.reserve(2 * KD)

            def scalar(self, act):
                for j in range(0, VT, 4):
                    w = min(4, VT - j) * P
                    act.activation(cols[:, j * P:j * P + w], ps[:, j // 4, 0:w], ACT.Copy)
                act.drain()
                act.activation(silu_c[:, :, 0], cols[:, row_of["c"]:row_of["c"] + KD], ACT.Silu)
                n = 0
                for dst, w in ((memT, MEM), (xT, SEQ)):
                    for k in range(KD):
                        act.wait_ge(turned_heads.sem, self.turn0 + n + 1)
                        act.activation(dst[:, k, 0:w], ps[:, 4 + n % 4, 0:w], ACT.Copy).then_inc(highs.sem, 1)
                        n += 1

            def vector(self, dve):
                dve.wait_ge(tables_in, 16 * 7)
                dve.tensor_copy(angle[:, 0, :], pos_int[:, :])
                dve.drain()
                dve.tensor_scalar(angle[:, 0, :], angle[:, 0, :], rope_inv, None, ALU.mult)
                dve.drain()
                for n, quarter in ((1, 0.0), (2, 0.25)):
                    dve.tensor_scalar(angle[:, 3, :], angle[:, 0, :], 1.0 / (2.0 * math.pi), quarter, ALU.mult, ALU.add)
                    dve.drain()
                    dve.tensor_scalar(angle[:, 3, :], angle[:, 3, :], ROUND, None, ALU.add)
                    dve.drain()
                    dve.tensor_scalar(angle[:, 3, :], angle[:, 3, :], ROUND, None, ALU.subtract)
                    dve.drain()
                    dve.scalar_tensor_tensor(angle[:, n, :], angle[:, 3, :], -TWO_PI_HIGH, angle[:, 0, :], ALU.mult, ALU.add)
                    dve.drain()
                    dve.scalar_tensor_tensor(angle[:, n, :], angle[:, 3, :], -TWO_PI_LOW, angle[:, n, :], ALU.mult, ALU.add)
                    dve.drain()
                    dve.tensor_scalar(angle[:, n, :], angle[:, n, :], quarter * 2.0 * math.pi, math.pi * (1 - 2.0 ** -22), ALU.add, ALU.min)
                    dve.drain()
                    dve.tensor_scalar(angle[:, n, :], angle[:, n, :], -math.pi * (1 - 2.0 ** -22), None, ALU.max)
                    dve.drain()
                for n in range(2):
                    dve.tensor_tensor_reduce(out=tmpA[:, n, 0:DH], in0=lams[:, 2 * n, :], in1=lams[:, 2 * n + 1, :], scale=1.0,
                                             scalar=0.0, op0=ALU.mult, op1=ALU.add, accum_out=dots[:, n:n + 1])

        class Sines(Stage):
            def scalar(self, act):
                act.activation(sinT[:, :], angle[:, 1, :], ACT.Sin)
                act.activation(cosT[:, :], angle[:, 2, :], ACT.Sin)
                act.activation(dot_exp, dots, ACT.Exp)

        class Lambda(Stage):
            def vector(self, dve):
                dve.tensor_scalar(sinT[:, :], sinT[:, :], rope_sign, None, ALU.mult)
                dve.tensor_tensor(neg_lam, dot_exp[:, 1:2], dot_exp[:, 0:1], ALU.subtract)
                dve.drain()
                dve.tensor_scalar(neg_lam, neg_lam, LAMBDA_INIT, None, ALU.subtract)
                dve.memset(v_pad[:, :, 0:TAPS - 1], 0.0)

        class Modulation:
            def __init__(self):
                self.after = len(stages)
                self.formed0, self.taken0 = mod_formed.reserve(8), mod_taken.reserve(8)
                runs.append(self)

            def load(self, sp):
                sp.wait_ge(tensor_done, self.after)
                for l in range(2):
                    for i in turns(sp, 4):
                        for k in range(KD):
                            u = k % MOD_SLOTS
                            sp.wait_ge(mod_free[u], i * 2 + (8 * l + k // MOD_SLOTS + 1))
                            alone(sp, i)
                            w_rows = a["w_mod_2"][l][k * P:k * P + P, :]
                            sp.dma_start(mod_ring[:, u, :], w_rows[:, bass.ds(i * MOD_STRIP, MOD_STRIP)]).then_inc(mod_landed[u], 16)

            def split(self, pool):
                pass

            def multiply(self, pe):
                for i in turns(pe, 4):
                    for bank in range(2):
                        pe.wait_ge(mod_taken.sem, i * 2 + (self.taken0 + bank - 1))
                        alone(pe, i)
                        for k in range(KD):
                            u = k % MOD_SLOTS
                            pe.wait_ge(mod_landed[u], i * 64 + 16 * (2 * bank + k // MOD_SLOTS + 1))
                            alone(pe, i)
                            for g in range(3):
                                last = pe.matmul(ps[GROUP * g:GROUP * g + GROUP, bank, :], silu_c[:, k, :], mod_ring[:, u, g * SEQ:g * SEQ + SEQ],
                                                 start=(k == 0), stop=(k == KD - 1))
                            last.then_inc(mod_free[u], 1)
                        pe.drain().then_inc(mod_formed.sem, 1)

            def take(self, act):
                for i in turns(act, 4):
                    for bank in range(2):
                        act.wait_ge(mod_formed.sem, i * 2 + (self.formed0 + bank + 1))
                        alone(act, i)
                        act.activation(at(mod_rows[0:3 * GROUP], i * 2 + bank), ps[0:3 * GROUP, bank, :], ACT.Copy).then_inc(mod_taken.sem, 1)

        class Conv(Stage):
            def __init__(self, modulation):
                super().__init__()
                self.modulation = modulation

            def tensor(self, pe):
                self.modulation.multiply(pe)

            def scalar(self, act):
                self.modulation.take(act)

            def vector(self, dve):
                for j in turns(dve, NCONV // 2):
                    two = [j * 2, j * 2 + 1]
                    for j2 in two:
                        dve.tensor_scalar(at(y, j2), at(v_pad, j2, 0, SEQ), col("w_dw_a", j2), col("b_dw_a", j2), ALU.mult, ALU.add)
                    dve.drain()
                    for t in range(1, TAPS):
                        for j2 in two:
                            dve.scalar_tensor_tensor(at(y, j2), at(v_pad, j2, t, t + SEQ), col("w_dw_a", j2 + t * NCONV), at(y, j2),
                                                     ALU.mult, ALU.add)
                        dve.drain()

        class ModTurn(Stage):
            def tensor(self, pe):
                w = 3 * GROUP
                for b in range(32):
                    pe.transpose(ps[:, b // 4, b % 4 * w:b % 4 * w + w], mod_rows[0:w, b // 4, b % 4 * P:b % 4 * P + P], ident[0:w, 0:w])

        class ModBias(Stage):
            def vector(self, dve):
                turned = ps[:, :, 0:12 * GROUP].rearrange("p j (c g q) -> p j c g q", c=4, q=GROUP)
                bias = cols[:, row_of["b_mod"]:row_of["b_mod"] + 96].rearrange("p (j g c) -> p j g c", j=8, g=3)
                to = mod[:, :].rearrange("p (j g c) -> p j g c", j=8, g=3)
                for g in range(3):
                    dve.tensor_tensor(to[:, :, g, :], turned[:, :, :, g, 0], bias[:, :, g, :], ALU.add)
                dve.drain()
                dve.tensor_scalar(mod_plus[:, :], mod[:, :], 1.0, None, ALU.add)

        class LayerNorm(Stage):
            def __init__(self, buf, tiles, gname, bname, k0=0, silu=False):
                super().__init__()
                self.buf, self.tiles, self.gname, self.bname, self.k0, self.silu = buf, tiles, gname, bname, k0, silu
                self.sum0, self.root0 = sums_in.reserve(1), roots.reserve(2)
                self.centred0, self.square0, self.summed0 = centred.reserve(tiles), squares.reserve(tiles), summed.reserve(tiles)
                self.part0 = parts.reserve(tiles)
                if silu:
                    self.high0, self.low0 = highs.reserve(tiles), lows.reserve(tiles)

            def tensor(self, pe):
                for k in range(self.tiles):
                    pe.matmul(ps[:, 6, :], ones[:, :], self.buf[:, k, :], start=(k == 0), stop=(k == self.tiles - 1))
                pe.drain().then_inc(sums_in.sem, 1)
                square_sum(pe, self.square0, 7, self.tiles, SEQ)

            def scalar(self, act):
                width = 1.0 / (self.tiles * P)
                act.wait_ge(sums_in.sem, self.sum0 + 1)
                act.activation(mean[:, :], ps[:, 6, :], ACT.Copy, scale=width).then_inc(roots.sem, 1)
                square_tiles(act, self.buf, self.square0, self.summed0, self.tiles, SEQ, self.centred0)
                act.wait_ge(summed.sem, self.summed0 + self.tiles)
                act.activation(mean[:, :], ps[:, 7, :], ACT.Sqrt, bias=eps_ln, scale=width).then_inc(roots.sem, 1)
                for k in range(self.tiles):
                    act.wait_ge(parts.sem, self.part0 + k + 1)
                    if self.silu:
                        act.wait_ge(lows.sem, self.low0 + k - 3)
                        act.activation(tmpB[:, k % 4, :], self.buf[:, k, :], ACT.Silu, bias=col(self.bname, self.k0 + k))
                        act.drain()
                        act.activation(hH[:, k, :], tmpB[:, k % 4, :], ACT.Copy).then_inc(highs.sem, 1)
                    else:
                        act.activation(self.buf[:, k, :], self.buf[:, k, :], ACT.Identity, bias=col(self.bname, self.k0 + k))

            def vector(self, dve):
                dve.wait_ge(roots.sem, self.root0 + 1)
                for k in range(self.tiles):
                    dve.tensor_tensor(self.buf[:, k, :], self.buf[:, k, :], mean[:, :], ALU.subtract).then_inc(centred.sem, 1)
                dve.wait_ge(roots.sem, self.root0 + 2)
                dve.reciprocal(rstd[:, :], mean[:, :])
                dve.drain()
                for k in range(self.tiles):
                    dve.scalar_tensor_tensor(self.buf[:, k, :], self.buf[:, k, :], col(self.gname, self.k0 + k), rstd[:, :],
                                             ALU.mult, ALU.mult).then_inc(parts.sem, 1)
                if self.silu:
                    for k in range(self.tiles):
                        dve.wait_ge(highs.sem, self.high0 + k + 1)
                        dve.tensor_tensor(hL[:, k, :], tmpB[:, k % 4, :], hH[:, k, :].bitcast(F32), ALU.subtract).then_inc(lows.sem, 1)

        class FinalRms(Stage):
            def __init__(self):
                super().__init__()
                self.square0, self.summed0, self.root0 = squares.reserve(KD), summed.reserve(KD), roots.reserve(1)

            def tensor(self, pe):
                square_sum(pe, self.square0, 7, KD, SEQ)

            def scalar(self, act):
                square_tiles(act, xT, self.square0, self.summed0, KD, SEQ)
                act.wait_ge(summed.sem, self.summed0 + KD)
                act.activation(mean[:, :], ps[:, 7, :], ACT.Sqrt, bias=eps_rms, scale=1.0 / D).then_inc(roots.sem, 1)

            def vector(self, dve):
                dve.wait_ge(roots.sem, self.root0 + 1)
                dve.reciprocal(rstd[:, :], mean[:, :])
                dve.drain()
                for k in range(KD):
                    dve.scalar_tensor_tensor(xT[:, k, :], xT[:, k, :], col("g_final", k), rstd[:, :], ALU.mult, ALU.mult)

        class Attend(Stage):
            def __init__(self, q, k, v, pairs, k0=0, v0=0, keys=SEQ, masked=True, bias=None, shared=False, mix=False):
                super().__init__()
                self.q, self.k, self.v, self.pairs, self.k0, self.v0, self.keys = q, k, v, pairs, k0, v0, keys
                self.masked, self.bias, self.shared, self.mix = masked, bias, shared, mix
                self.dv = 2 * DH if mix else DH
                units = 8 * pairs
                self.staged0 = staged.reserve(pairs)
                self.logits0, self.turned0, self.value0 = logits_in.reserve(units), turned_in.reserve(units), value_in.reserve(units)
                self.max0, self.exp0, self.out0 = max_in.reserve(units), exp_in.reserve(units), head_out.reserve(units)
                self.tact0, self.tdve0 = turned_act.reserve(units // 2), turned_dve.reserve(units // 2)

            def unit(self, s):
                qt = s % 4
                return s // 8, s // 4 % 2, qt, (qt + 1) * P if self.masked else self.keys

            def turned_wait(self, eng, i, s):
                if s % 4 < 2:
                    eng.wait_ge(turned_act.sem, i * 8 + (self.tact0 + s // 4 * 2 + s % 4 + 1))
                    alone(eng, i)
                else:
                    eng.wait_ge(turned_dve.sem, i * 8 + (self.tdve0 + s // 4 * 2 + s % 4 - 1))
                    alone(eng, i)

            def tensor(self, pe):
                for i in turns(pe, self.pairs // 2):
                    for s in range(16 + 3):
                        if s < 16:
                            p, hh, qt, seen = self.unit(s)
                            if s % 8 == 0:
                                pe.wait_ge(staged.sem, i * 2 + (self.staged0 + p + 1))
                                alone(pe, i)
                            pe.wait_ge(exp_in.sem, i * 16 + (self.exp0 + s - 3))
                            alone(pe, i)
                            lo = hh * DH
                            keys = self.k[lo:lo + DH, self.k0, 0:seen] if self.shared else kS[lo:lo + DH, p, 0:seen]
                            mm = pe.matmul(ps[:, s % 4, 0:seen], qS[lo:lo + DH, p, qt * P:qt * P + P], keys,
                                           start=True, stop=True)
                            if self.masked and self.bias != "chosen":
                                mm = pe.matmul(ps[:, s % 4, seen - P:seen], identR[:, :], causalR[:, :], start=False, stop=True,
                                               skip_group_check=True)
                            mm.then_inc(logits_in.sem, 1)
                        if 2 <= s < 18:
                            t = s - 2
                            p, hh, qt, seen = self.unit(t)
                            pe.wait_ge(exp_in.sem, i * 16 + (self.exp0 + t + 1))
                            alone(pe, i)
                            self.turned_wait(pe, i, t - 2)
                            for k in range(seen // P):
                                mm = pe.transpose(ps[:, 4 + t % 2, k * P:k * P + P], tmpA[:, t % 4, k * P:k * P + P], ident[:, :])
                            mm.then_inc(turned_in.sem, 1)
                        if s >= 3:
                            t = s - 3
                            p, hh, qt, seen = self.unit(t)
                            self.turned_wait(pe, i, t)
                            pe.wait_ge(head_out.sem, i * 16 + (self.out0 + t - 1))
                            alone(pe, i)
                            for k in range(seen // P):
                                values = self.value(i, p, hh, k)
                                mm = pe.matmul(ps[:, 6 + t % 2, 0:self.dv], tmpB[:, t % 2, k * P:k * P + P], values,
                                               start=(k == 0), stop=(k == seen // P - 1))
                            mm.then_inc(value_in.sem, 1)

            def value(self, i, p, hh, k):
                if self.shared:
                    return self.v[:, k, 0:DH]
                lo = i * (4 * DH) + (p * 2 * DH + (0 if self.mix else hh * DH))
                return at(self.v, self.v0 + k, lo, lo + self.dv) if isinstance(lo, int) \
                    else self.v[:, self.v0 + k, bass.ds(lo, self.dv)]

            def stage(self, act, i, p):
                act.wait_ge(logits_in.sem, i * 16 + (self.logits0 + 8 * p - 8))
                alone(act, i)
                act.activation(qS[:, p, :], at(self.q, i * 2 + p), ACT.Copy, scale=SCALE)
                if not self.shared:
                    act.activation(kS[:, p, 0:self.keys], at(self.k, i * 2 + (p + self.k0), 0, self.keys), ACT.Copy)
                if self.bias == "gates":
                    for hh in range(2):
                        act.activation(gateS[:, 2 * p + hh, :], at(gate_rows, i * 4 + (2 * p + hh)), ACT.Copy)
                act.drain().then_inc(staged.sem, 1)

            def scalar(self, act):
                for i in turns(act, self.pairs // 2):
                    self.stage(act, i, 0)
                    self.stage(act, i, 1)
                    for s in range(16 + 2):
                        if s < 16:
                            p, hh, qt, seen = self.unit(s)
                            act.wait_ge(max_in.sem, i * 16 + (self.max0 + s + 1))
                            alone(act, i)
                            act.wait_ge(turned_in.sem, i * 16 + (self.turned0 + s - 3))
                            alone(act, i)
                            src = tmpA[:, s % 4, 0:seen] if self.bias else ps[:, s % 4, 0:seen]
                            act.activation(tmpA[:, s % 4, 0:seen], src, ACT.Exp, bias=neg_max[:, s:s + 1],
                                           scale=-1.0 if self.bias else 1.0, accum_out=row_sum[:, s:s + 1]).then_inc(exp_in.sem, 1)
                        if s >= 2 and s % 4 >= 2:
                            t = s - 2
                            p, hh, qt, seen = self.unit(t)
                            act.wait_ge(turned_in.sem, i * 16 + (self.turned0 + t + 1))
                            alone(act, i)
                            act.wait_ge(value_in.sem, i * 16 + (self.value0 + t - 1))
                            alone(act, i)
                            act.activation(tmpB[:, t % 2, 0:seen], ps[:, 4 + t % 2, 0:seen], ACT.Copy).then_inc(turned_act.sem, 1)

            def vector(self, dve):
                for i in turns(dve, self.pairs // 2):
                    for s in range(16 + 3):
                        if s < 16:
                            p, hh, qt, seen = self.unit(s)
                            dve.wait_ge(logits_in.sem, i * 16 + (self.logits0 + s + 1))
                            alone(dve, i)
                            m = neg_max[:, s:s + 1]
                            if self.bias:
                                dve.wait_ge(turned_in.sem, i * 16 + (self.turned0 + s - 3))
                                alone(dve, i)
                                row = chosen[:, qt, 0:seen] if self.bias == "chosen" else gateS[:, 2 * p + hh, 0:seen]
                                dve.tensor_tensor_reduce(out=tmpA[:, s % 4, 0:seen], in0=ps[:, s % 4, 0:seen], in1=row, scale=-1.0,
                                                         scalar=-LOWEST, op0=ALU.add, op1=ALU.min, accum_out=m).then_inc(max_in.sem, 1)
                            else:
                                dve.tensor_reduce(m, ps[:, s % 4, 0:seen], AX.X, ALU.max, negate=True).then_inc(max_in.sem, 1)
                        if 2 <= s < 18 and (s - 2) % 4 >= 2:
                            t = s - 2
                            p, hh, qt, seen = self.unit(t)
                            dve.wait_ge(turned_in.sem, i * 16 + (self.turned0 + t + 1))
                            alone(dve, i)
                            dve.wait_ge(value_in.sem, i * 16 + (self.value0 + t - 1))
                            alone(dve, i)
                            dve.tensor_copy(tmpB[:, t % 2, 0:seen], ps[:, 4 + t % 2, 0:seen]).then_inc(turned_dve.sem, 1)
                        if s >= 3:
                            t = s - 3
                            p, hh, qt, seen = self.unit(t)
                            dve.wait_ge(value_in.sem, i * 16 + (self.value0 + t + 1))
                            alone(dve, i)
                            inv = row_inv[:, t:t + 1]
                            dve.reciprocal(inv, row_sum[:, t:t + 1])
                            dve.drain()
                            lo = qt * P + (0 if self.mix else hh * DH)
                            to, o = at(self.q, i * 2 + p, lo, lo + self.dv), ps[:, 6 + t % 2, 0:self.dv]
                            if self.mix and hh:
                                dve.tensor_scalar(inv, inv, neg_lam, None, ALU.mult)
                                dve.drain()
                                dve.scalar_tensor_tensor(to, o, inv, to, ALU.mult, ALU.add).then_inc(head_out.sem, 1)
                            else:
                                dve.tensor_scalar(to, o, inv, None, ALU.mult).then_inc(head_out.sem, 1)

        class GateLogs(Stage):
            def scalar(self, act):
                act.activation(tmpA[0:FOX, 0, :], gate[0:FOX, :], ACT.Abs)
                act.drain()
                act.activation(tmpA[0:FOX, 0, :], tmpA[0:FOX, 0, :], ACT.Exp, scale=-1.0)
                act.drain()
                act.activation(tmpA[0:FOX, 1, :], tmpA[0:FOX, 0, :], ACT.Ln, bias=1.0)

            def vector(self, dve):
                dve.memset(tmpB[0:FOX, 0, :], 1.0)

        class GateSums(Stage):
            def vector(self, dve):
                dve.scalar_tensor_tensor(tmpB[0:FOX, 1, :], gate[0:FOX, :], 0.0, tmpA[0:FOX, 1, :], ALU.min, ALU.subtract)
                dve.drain()
                dve.tensor_tensor_scan(gate[0:FOX, :], tmpB[0:FOX, 0, :], tmpB[0:FOX, 1, :], 0.0, ALU.mult, ALU.add)

        class GateRows(Stage):
            def __init__(self):
                super().__init__()
                self.turn0, self.high0 = turned_heads.reserve(FOX), highs.reserve(FOX)

            def tensor(self, pe):
                for h in range(FOX):
                    pe.wait_ge(highs.sem, self.high0 + h - 3)
                    pe.matmul(ps[:, h % 4, :], pick[0:FOX, h, :], gate[0:FOX, :], start=True, stop=True).then_inc(turned_heads.sem, 1)

            def scalar(self, act):
                for h in range(FOX):
                    act.wait_ge(turned_heads.sem, self.turn0 + h + 1)
                    act.activation(gate_rows[:, h, :], ps[:, h % 4, :], ACT.Copy, scale=-1.0).then_inc(highs.sem, 1)

        class Pick(Stage):
            def vector(self, dve):
                for h in range(FOX):
                    dve.tensor_scalar(pick[:, h, :], ones[:, :], ident[:, h:h + 1], None, ALU.mult)

        class Choose(Stage):
            def __init__(self):
                super().__init__()
                units = IDX * (QT - 1)
                self.index0, self.relu0, self.used0 = index_in.reserve(units), relus.reserve(units), scored.reserve(units)
                self.units = [(h, qt) for h in range(IDX) for qt in range(1, QT)]

            def tensor(self, pe):
                for n, (h, qt) in enumerate(self.units):
                    pe.wait_ge(relus.sem, self.relu0 + n - 3)
                    lo, seen = h % 2 * DH, (qt + 1) * P
                    pe.matmul(ps[:, n % 4, 0:seen], ixQ[lo:lo + DH, h // 2, qt * P:qt * P + P], spK[lo:lo + DH, 1, 0:seen],
                              start=True, stop=True).then_inc(index_in.sem, 1)

            def scalar(self, act):
                for n, (h, qt) in enumerate(self.units):
                    seen = (qt + 1) * P
                    act.wait_ge(index_in.sem, self.index0 + n + 1)
                    act.wait_ge(scored.sem, self.used0 + n - 3)
                    act.activation(tmpA[:, n % 4, 0:seen], ps[:, n % 4, 0:seen], ACT.Relu, scale=SCALE).then_inc(relus.sem, 1)

            def vector(self, dve):
                dve.tensor_copy(chosen[:, 0, 0:P], causal[:, :])
                dve.tensor_scalar(spV[:, :, DH:DH + IDX], spV[:, :, DH:DH + IDX], IDX ** -0.5, None, ALU.mult)
                dve.drain()
                for n, (h, qt) in enumerate(self.units):
                    seen = (qt + 1) * P
                    dve.wait_ge(relus.sem, self.relu0 + n + 1)
                    weight, to = spV[:, qt, DH + h:DH + h + 1], chosen[:, qt, 0:seen]
                    if h == 0:
                        dve.tensor_scalar(to, tmpA[:, n % 4, 0:seen], weight, None, ALU.mult).then_inc(scored.sem, 1)
                    else:
                        dve.scalar_tensor_tensor(to, tmpA[:, n % 4, 0:seen], weight, to, ALU.mult, ALU.add).then_inc(scored.sem, 1)
                    dve.drain()
                for qt in range(1, QT):
                    mine = chosen[:, qt, qt * P:qt * P + P]
                    dve.tensor_tensor(mine, mine, causal[:, :], ALU.add)
                dve.drain()
                for r in turns(dve, TOPK // 8):
                    for qt in range(1, QT):
                        dve.max(top8[:, qt - 1, :], chosen[:, qt, 0:(qt + 1) * P])
                    dve.drain()
                    for qt in range(1, QT):
                        t = chosen[:, qt, 0:(qt + 1) * P]
                        dve.match_replace(t, top8[:, qt - 1, :], t, TAKEN)
                    dve.drain()
                for qt in range(1, QT):
                    t = chosen[:, qt, 0:(qt + 1) * P]
                    dve.tensor_scalar(t, t, LOWEST, MASKED, ALU.is_gt, ALU.mult)

        class Stick(Stage):
            FIRST = [0, 512, 896, 1152]

            def __init__(self):
                super().__init__()
                self.staged0, self.z0, self.log0, self.keep0 = staged.reserve(4), stick_z.reserve(32), stick_log.reserve(8), stick_keep.reserve(8)
                self.sum0, self.wt0, self.pv0, self.out0 = stick_sum.reserve(8), stick_wt.reserve(8), stick_pv.reserve(8), stick_out.reserve(8)

            def tensor(self, pe):
                for i in turns(pe, 4):
                    pe.wait_ge(staged.sem, i + (self.staged0 + 1))
                    alone(pe, i)
                    pe.wait_ge(stick_out.sem, i * 2 + self.out0)
                    alone(pe, i)
                    for hh in range(2):
                        lo = hh * DH
                        for k in range(QT):
                            n = SEQ - k * P
                            bank = ps[:, 4 * hh + k, :]
                            pe.matmul(bank[:, 0:n], stickK[lo:lo + DH, k * P:k * P + P], stickQ[lo:lo + DH, k * P:SEQ],
                                      start=True, stop=True)
                            pe.matmul(bank[:, 0:P], identR[:, :], beforeR[:, :], start=False, stop=True, skip_group_check=True
                                      ).then_inc(stick_z.sem, 1)
                    for hh in range(2):
                        pe.wait_ge(stick_keep.sem, i * 2 + (self.keep0 + hh + 1))
                        alone(pe, i)
                        for k in range(QT):
                            n = SEQ - k * P
                            for k2 in range(k, QT):
                                m = SEQ - k2 * P
                                mm = pe.matmul(ps[:, 4 * hh + k, n - m:n], (neg_tri if k2 == k else neg_ones)[:, :],
                                               keep[:, hh, self.FIRST[k2]:self.FIRST[k2] + m], start=False, stop=True, skip_group_check=True)
                        mm.then_inc(stick_sum.sem, 1)
                    for hh in range(2):
                        pe.wait_ge(stick_wt.sem, i * 2 + (self.wt0 + hh + 1))
                        alone(pe, i)
                        lo = i * (2 * DH) + hh * DH
                        for qt in range(QT):
                            for k in range(qt + 1):
                                w0 = self.FIRST[k] + (qt - k) * P
                                pe.matmul(ps[:, 4 * hh + 3, 256 + qt * DH:256 + qt * DH + DH], stick_w[:, hh, w0:w0 + P],
                                          stV[:, k, bass.ds(lo, DH)], start=(k == 0), stop=(k == qt))
                        pe.drain().then_inc(stick_pv.sem, 1)

            def scalar(self, act):
                for i in turns(act, 4):
                    act.wait_ge(stick_z.sem, i * 8 + self.z0)
                    alone(act, i)
                    act.activation(stickQ[:, :], at(stQ, i), ACT.Copy, scale=SCALE)
                    act.activation(stickK[:, :], at(stK, i), ACT.Copy)
                    act.drain().then_inc(staged.sem, 1)
                    for hh in range(2):
                        act.wait_ge(stick_pv.sem, i * 2 + (self.pv0 + hh - 1))
                        alone(act, i)
                        e = stick_w[:, hh, :]
                        for k in range(QT):
                            n = SEQ - k * P
                            act.wait_ge(stick_z.sem, i * 8 + (self.z0 + 4 * hh + k + 1))
                            alone(act, i)
                            act.activation(e[:, self.FIRST[k]:self.FIRST[k] + n], ps[:, 4 * hh + k, 0:n], ACT.Abs)
                        act.drain()
                        act.activation(e, e, ACT.Exp, scale=-1.0)
                        act.drain()
                        act.activation(e, e, ACT.Ln, bias=1.0).then_inc(stick_log.sem, 1)
                    for hh in range(2):
                        act.wait_ge(stick_sum.sem, i * 2 + (self.sum0 + hh + 1))
                        alone(act, i)
                        for k in range(QT):
                            n = SEQ - k * P
                            last = act.activation(stick_w[:, hh, self.FIRST[k]:self.FIRST[k] + n], ps[:, 4 * hh + k, 0:n], ACT.Exp)
                        last.then_inc(stick_wt.sem, 1)

            def vector(self, dve):
                for i in turns(dve, 4):
                    for hh in range(2):
                        dve.wait_ge(stick_log.sem, i * 2 + (self.log0 + hh + 1))
                        alone(dve, i)
                        for k in range(QT):
                            n = SEQ - k * P
                            f = self.FIRST[k]
                            last = dve.scalar_tensor_tensor(keep[:, hh, f:f + n], ps[:, 4 * hh + k, 0:n], 0.0, stick_w[:, hh, f:f + n],
                                                            ALU.max, ALU.add)
                        last.then_inc(stick_keep.sem, 1)
                    for hh in range(2):
                        dve.wait_ge(stick_pv.sem, i * 2 + (self.pv0 + hh + 1))
                        alone(dve, i)
                        to = at(stQ, i).rearrange("p (t c) -> p t c", t=QT)[:, :, hh * DH:hh * DH + DH]
                        dve.tensor_copy(to, ps[:, 4 * hh + 3, 256:512].rearrange("p (t c) -> p t c", t=QT)).then_inc(stick_out.sem, 1)

        class SubNorm(Stage):
            def __init__(self):
                super().__init__()
                self.square0, self.root0 = squares.reserve(8), roots.reserve(1)
                self.low0 = lows.reserve(8)

            def scalar(self, act):
                for h in range(8):
                    act.wait_ge(lows.sem, self.low0 + h - 3)
                    act.activation(tmpA[:, h % 4, :], difQ[:, h, :], ACT.Square).then_inc(squares.sem, 1)
                act.wait_ge(lows.sem, self.low0 + 8)
                act.activation(head_std, head_sq, ACT.Sqrt, bias=eps_ln, scale=1.0 / P).then_inc(roots.sem, 1)

            def vector(self, dve):
                for h in range(8):
                    dve.wait_ge(squares.sem, self.square0 + h + 1)
                    dve.tensor_reduce(head_sq[:, 4 * h:4 * h + 4], tmpA[:, h % 4, :].rearrange("p (t c) -> p t c", t=QT), AX.X, ALU.add
                                      ).then_inc(lows.sem, 1)
                dve.wait_ge(roots.sem, self.root0 + 1)
                dve.reciprocal(head_sq, head_std)
                dve.drain()
                for n in range(32):
                    t = difQ[:, n // 4, n % 4 * P:n % 4 * P + P]
                    dve.tensor_scalar(t, t, head_sq[:, n:n + 1], None, ALU.mult)
                g = cols[:, row_of["subln"]:row_of["subln"] + 1]
                dve.tensor_scalar(g, g, 1.0 - LAMBDA_INIT, None, ALU.mult)

        class Output(Stage):
            def __init__(self):
                super().__init__()
                self.turn0, self.high0 = turned_heads.reserve(KD), highs.reserve(KD)

            def tensor(self, pe):
                for n in range(KD):
                    pe.wait_ge(highs.sem, self.high0 + n - 3)
                    t, h = n // 2, n % 2
                    for k in range(4):
                        pe.transpose(ps[:, n % 4, k * P:k * P + P], xT[:, 4 * h + k, t * P:t * P + P], ident[:, :])
                    pe.drain().then_inc(turned_heads.sem, 1)

            def scalar(self, act):
                for n in range(KD):
                    act.wait_ge(turned_heads.sem, self.turn0 + n + 1)
                    act.activation(tok_out[:, n // 2, n % 2 * 512:n % 2 * 512 + 512], ps[:, n % 4, :], ACT.Copy).then_inc(highs.sem, 1)

        Constants()
        Tables()
        Sines()
        mem_w = a["w_mem_kv"]
        Products(RmsParts(memT, "g_mem", n=MEM),
                 *[Run("A", 1, KD, plain(mem_w[l]), TakeCopy(memK, MEM, 2 * l), tokens=MEM) if kind == "k" else
                   Run("B", 1, KD, plain(mem_w[l], MEM), TakeMemV(l), tokens=MEM) for l in range(2) for kind in "kv"])
        Lambda()
        w = a["w_in_a"][0]
        Products(RmsParts(xT, "g_mix", 0),
                 Run("A", NCONV, KD, pairs_of(w, 0, w, CONV), TakeGlu()),
                 Run("A", 1, KD, plain(w, 2 * CONV), TakeCopy(q_mem0)))
        modulation = Modulation()
        Attend(q_mem0, memK, memV, 2, k0=0, v0=0, keys=MEM, masked=False)
        Conv(modulation)
        ModTurn()
        ModBias()
        LayerNorm(y, NCONV, "ln_g", "ln_b", silu=True)
        Products(HeadParts([(q_mem0, 0), (q_mem0, 1)], first=NCONV), Run("A", 4, KD, plain(a["w_out"][0]), TakeResidual()))

        def conv_ff(l):
            FeedForward(RmsParts(xT, "g_ffn", KD * l), lambda h: pairs_of(a["w_up"][l], h * HALF * P, a["w_up"][l], FF + h * HALF * P),
                        a["w_down"][l], conv=l)
        conv_ff(0)
        w = a["w_kvf"]
        Products(RmsParts(xT, "g_kv"),
                 Run("A", 3, KD, plain(w), TakeCopy(foxK)),
                 Run("B", 3, KD, plain(w, CONV), TakeValues(foxV)),
                 Run("A", 1, KD, lambda s: [(0, FOX, columns(w, 2 * CONV, FOX)), (FOX, P, columns(w, 0, P - FOX))],
                     TakeForget(), width=P))
        w_b = a["w_in_b"][0]
        Products(RmsParts(xT, "g_mix", KD, again=True),
                 Run("A", 3, KD, plain(w_b), TakeCopy(foxQ)),
                 Run("A", 1, KD, plain(w_b, CONV), TakeCopy(q_mem1)))
        GateLogs()
        GateSums()
        Pick()
        GateRows()
        Attend(foxQ, foxK, foxV, 6, bias="gates")
        Attend(q_mem1, memK, memV, 2, k0=2, v0=2, keys=MEM, masked=False)
        Products(HeadParts([(foxQ, t) for t in range(6)] + [(q_mem1, 0), (q_mem1, 1)]),
                 Run("A", 4, KD, plain(a["w_out"][1]), TakeResidual()))
        conv_ff(1)
        FinalRms()

        def gain(l, chunk):
            return 48 * l + KD * chunk

        def gated_ff(l):
            FeedForward(ModParts(l, 3, 4), lambda h: pairs_of(a["w_gate_2"][l], h * HALF * P, a["w_up_2"][l], h * HALF * P),
                        a["w_down_2"][l], gain=gain(l, 5))
            LayerNorm(xT, KD, "ln_ffn_g", "ln_ffn_b", KD * l)
        w_e = a["w_in_even_2"][0]
        Products(ModParts(0, 0, 1),
                 Run("A", 2, KD, plain(w_e, 0), TakeCopy(stQ)),
                 Run("A", 2, KD, plain(w_e, 512), TakeCopy(stK)),
                 Run("B", 2, KD, plain(w_e, 1024), TakeValues(stV)),
                 Run("A", 2, KD, plain(w_e, 1536), TakeRope(spQ)),
                 Run("A", 1, KD, lambda s: [(0, 64, columns(w_e, 2048, 64)), (64, 128, columns(w_e, 2048, 64)),
                                            (128, 192, columns(w_e, 2432, 64)), (192, 256, columns(w_e, 2432, 64))],
                     TakeRope(spK), npieces=4),
                 Run("A", 1, KD, plain(w_e, 2176), TakeRope(ixQ)),
                 Run("B", 1, KD, lambda s: [(0, 64, columns(w_e, 2112, 64)), (64, 68, columns(w_e, 2496, 4))],
                     TakeValues(spV), width=68))
        Choose()
        Stick()
        Attend(spQ, spK, spV, 4, bias="chosen", shared=True)
        Products(HeadParts([(stQ, t) for t in range(4)] + [(spQ, t) for t in range(4)]),
                 Run("A", 4, KD, plain(a["w_out_even_2"][0]), TakeResidual(gain(0, 2))))
        LayerNorm(xT, KD, "ln_mix_g", "ln_mix_b", 0)
        gated_ff(0)
        w_o = a["w_in_odd_2"][0]
        Products(ModParts(1, 0, 1),
                 Run("A", 4, KD, plain(w_o, 0), TakeRope(difQ)),
                 Run("A", 4, KD, plain(w_o, D), TakeRope(difK)),
                 Run("B", 4, KD, plain(w_o, 2 * D), TakeValues(difV)))
        Attend(difQ, difK, difV, 8, mix=True)
        SubNorm()
        Products(HeadParts([(difQ, t) for t in range(8)], gain=col("subln", 0)),
                 Run("A", 4, KD, plain(a["w_out_odd_2"][0]), TakeResidual(gain(1, 2))))
        LayerNorm(xT, KD, "ln_mix_g", "ln_mix_b", KD)
        gated_ff(1)
        Output()

        vector_loads = []
        for name, v in vectors:
            r0, n = row_of[name], v.shape[0]
            while n:
                m = min(n, P - r0 % P)
                k = r0 - row_of[name]
                vector_loads.append((vec_rows[r0 % P:r0 % P + m, r0 // P, :], v[k:k + m, :]))
                r0, n = r0 + m, n - m

        for name in ("pe", "act", "dve", "pool", "sp"):
            turn[name] = sem(name + "_turn")
        block = ctx.enter_context(nc.Block())

        @block.sync
        def _(sp):
            turn[id(sp)] = turn["sp"]
            sp.dma_start(tok_mem[:, :, :], a["mem"][0].rearrange("(t p) d -> p t d", p=P)).then_inc(tokens_in, 16)
            sp.dma_start(tok_x[:, :, :], a["x"][0].rearrange("(t p) d -> p t d", p=P)).then_inc(tokens_in, 16)
            sp.dma_start(rope_const, a["rope_const"]).then_inc(tables_in, 16)
            sp.dma_start(gate_bias[0:FOX, :], a["b_f"].rearrange("(h o) -> h o", o=1)).then_inc(tables_in, 16)
            sp.dma_start(pos_int[:, :], a["positions_2"][0].partition_broadcast(P)).then_inc(tables_in, 16)
            for n, name in enumerate(("lam_q1_2", "lam_k1_2", "lam_q2_2", "lam_k2_2")):
                sp.dma_start(lams[:, n, :], a[name][0].partition_broadcast(P)).then_inc(tables_in, 16)
            sp.wait_ge(constants_in, 1)
            for to, src in vector_loads:
                sp.dma_start(to, src).then_inc(vectors_in, 16)
            for run in runs:
                run.load(sp)
            sp.wait_ge(scalar_done, len(stages))
            sp.dma_start(out[0].rearrange("(t p) d -> p t d", p=P), tok_out[:, :, :]).then_inc(out_written, 16)
            sp.wait_ge(out_written, 16)

        @block.gpsimd
        def _(pool):
            turn[id(pool)] = turn["pool"]
            start_signals(pool, "pool")
            pool.sem_inc(raw_free[0], 1)
            pool.sem_inc(raw_free[1], 1)
            for free in mod_free:
                pool.sem_inc(free, 1)
            pool.memset(ident[:, :], 0.0)
            pool.memset(ones[:, :], 1.0)
            pool.memset(causal[:, :], 0.0)
            pool.memset(before[:, :], 0.0)
            pool.memset(neg_tri[:, :], -1.0)
            pool.memset(neg_ones[:, :], -1.0)
            pool.memset(silu_c[:, :, :], 0.0)
            pool.memset(vec_rows[:, VT - 1, :], 0.0)
            pool.drain()
            pool.affine_select(out=ident[:, :], in_=ident[:, :], compare_op=ALU.not_equal, fill=1.0, base=0,
                               pattern=[[-1, P]], channel_multiplier=1)
            pool.affine_select(out=causal[:, :], in_=causal[:, :], compare_op=ALU.is_ge, fill=MASKED, base=0,
                               pattern=[[-1, P]], channel_multiplier=1)
            pool.affine_select(out=before[:, :], in_=before[:, :], compare_op=ALU.is_ge, fill=MASKED, base=-1,
                               pattern=[[1, P]], channel_multiplier=-1)
            pool.affine_select(out=neg_tri[:, :], in_=neg_tri[:, :], compare_op=ALU.is_ge, fill=0.0, base=0,
                               pattern=[[-1, P]], channel_multiplier=1)
            pool.drain().then_inc(constants_in, 1)
            for run in runs:
                run.split(pool)

        @block.tensor
        def _(pe):
            turn[id(pe)] = turn["pe"]
            start_signals(pe, "pe")
            for n, stage in enumerate(stages):
                if n:
                    pe.wait_ge(scalar_done, n)
                    pe.wait_ge(vector_done, n)
                stage.tensor(pe)
                pe.drain().then_inc(tensor_done, 1)

        @block.scalar
        def _(act):
            turn[id(act)] = turn["act"]
            start_signals(act, "act")
            for n, stage in enumerate(stages):
                if n:
                    act.wait_ge(tensor_done, n)
                    act.wait_ge(vector_done, n)
                stage.scalar(act)
                act.drain().then_inc(scalar_done, 1)

        @block.vector
        def _(dve):
            turn[id(dve)] = turn["dve"]
            start_signals(dve, "dve")
            for n, stage in enumerate(stages):
                if n:
                    dve.wait_ge(tensor_done, n)
                    dve.wait_ge(scalar_done, n)
                stage.vector(dve)
                dve.drain().then_inc(vector_done, 1)


_INS = ["x", "mem", "g_mix", "w_in_a", "b_glu", "w_dw_a", "b_dw_a", "ln_g", "ln_b", "g_kv", "w_kvf", "b_f", "w_in_b", "g_mem",
        "w_mem_kv", "w_out", "g_ffn", "w_up", "w_dw_f", "b_dw_f", "w_down", "g_final", "c_2", "positions_2", "w_mod_2",
        "b_mod_2", "w_in_even_2", "w_out_even_2", "w_in_odd_2", "lam_q1_2", "lam_k1_2", "lam_q2_2", "lam_k2_2",
        "subln_g_2", "w_out_odd_2", "ln_mix_g_2", "ln_mix_b_2", "w_gate_2", "w_up_2", "w_down_2", "ln_ffn_g_2", "ln_ffn_b_2"]


def kernel(**inputs):
    import numpy as np
    import concourse.bacc as bacc
    from concourse.bass_utils import run_bass_kernel_spmd

    nc = bacc.Bacc("TRN2", target_bir_lowering=False, num_devices=1)
    arrays = {name: np.ascontiguousarray(inputs[name]) for name in _INS}
    inverse = np.float32(10000.0) ** (-np.arange(0, DH, 2, dtype=np.float32) / np.float32(DH))
    lane = np.arange(P)
    arrays["rope_const"] = np.stack([inverse[lane % (DH // 2)], np.where(lane % DH < DH // 2, -1.0, 1.0)], axis=1).astype(np.float32)
    aps = {name: nc.dram_tensor(name, v.shape, mybir.dt.from_np(v.dtype), kind="ExternalInput").ap() for name, v in arrays.items()}
    out = nc.dram_tensor("out", (1, SEQ, D), F32, kind="ExternalOutput").ap()
    build(nc, aps, out)
    return run_bass_kernel_spmd(nc, [arrays], core_ids=[0]).results[0]["out"]
```

```python
import math
from contextlib import ExitStack

import concourse.bass as bass
from concourse import mybir

F32 = mybir.dt.float32
F32R = mybir.dt.float32r
I32 = mybir.dt.int32
ACT = mybir.ActivationFunctionType
ALU = mybir.AluOpType
AX = mybir.AxisListType

P = 128
D = 1024
KD = D // P
SEQ = 512
QT = SEQ // P
MEM = 256
DH = 64
CONV = 768
NCONV = CONV // P
TAPS = 31
FOX = CONV // DH
FF = 2816
FT = FF // P
HALF = FT // 2
TOPK = 128
IDX = 4
RMS_EPS = 1e-6
LN_EPS = 1e-5
ALPHA = 4.0 ** 0.25
LAMBDA_INIT = 0.8 - 0.6 * math.exp(-0.3)
SCALE = DH ** -0.5
MASKED = -(2.0 ** 100)
TAKEN = -3.4e38
LOWEST = -3.0e38
STRIP = 256
SLOT = HALF * STRIP
MOD_SLOTS = 4
MOD_STRIP = 3 * SEQ
GROUP = 32
TWO_PI_HIGH = 6.28125
TWO_PI_LOW = 2.0 * math.pi - TWO_PI_HIGH
ROUND = 1.5 * 2.0 ** 23
START = 16


def build(nc, a, out):
    ctx = ExitStack()
    with ctx:
        def sb(name, shape, dt=F32, where=ctx):
            return where.enter_context(nc.sbuf_tensor(name, shape, dt))

        xT = sb("xT", [P, KD, SEQ])
        raw = sb("raw", [P, 2, SLOT])
        wH = sb("wH", [P, 2, SLOT], F32R)
        wL = sb("wL", [P, 2, SLOT], F32R)
        ident = sb("ident", [P, P])
        identR = sb("identR", [P, P], F32R)
        ones = sb("ones", [P, P])
        mean_of = sb("mean_of", [P, P])
        causal = sb("causal", [P, P])
        causalR = sb("causalR", [P, P], F32R)
        before = sb("before", [P, P])
        beforeR = sb("beforeR", [P, P], F32R)
        neg_tri = sb("neg_tri", [P, P])
        neg_ones = sb("neg_ones", [P, P])
        memK = sb("memK", [P, 4, MEM])
        memV = sb("memV", [P, 4, MEM])
        cosT = sb("cosT", [P, SEQ])
        sinT = sb("sinT", [P, SEQ])
        acc = sb("acc", [P, SEQ])
        rstd = sb("rstd", [P, SEQ])
        tmpA = sb("tmpA", [P, 4, SEQ])
        tmpB = sb("tmpB", [P, 4, SEQ])
        small = sb("small", [P, 128])
        eps_rms, eps_ln = small[:, 0:1], small[:, 1:2]
        neg_lam, gate_bias = small[:, 2:3], small[:, 3:4]
        rope_const = small[:, 4:6]
        rope_inv, rope_sign = small[:, 4:5], small[:, 5:6]
        dots, dot_exp = small[:, 6:8], small[:, 8:10]
        spare = small[:, 10:11]
        neg_max, row_sum, row_inv = small[:, 16:32], small[:, 32:48], small[:, 48:64]
        head_sq, head_std = small[:, 64:96], small[:, 96:128]
        top8 = sb("top8", [P, 3, 8])
        lams = sb("lams", [P, 4, DH])
        mod = sb("mod", [P, 96])
        mod_plus = sb("mod_plus", [P, 96])
        silu_c = sb("silu_c", [P, KD, GROUP])

        def by_rows(v):
            return v.rearrange("l (n p) -> (l n) p", p=P)
        vectors = [
            ("g_mix", by_rows(a["g_mix"])), ("b_glu", by_rows(a["b_glu"])), ("b_dw_a", by_rows(a["b_dw_a"])),
            ("ln_g", by_rows(a["ln_g"])), ("ln_b", by_rows(a["ln_b"])),
            ("g_kv", a["g_kv"].rearrange("(n p) -> n p", p=P)), ("g_mem", a["g_mem"].rearrange("(n p) -> n p", p=P)),
            ("g_ffn", by_rows(a["g_ffn"])), ("g_final", a["g_final"].rearrange("(n p) -> n p", p=P)),
            ("c", by_rows(a["c_2"])), ("subln", a["subln_g_2"]),
            ("ln_mix_g", by_rows(a["ln_mix_g_2"])), ("ln_mix_b", by_rows(a["ln_mix_b_2"])),
            ("ln_ffn_g", by_rows(a["ln_ffn_g_2"])), ("ln_ffn_b", by_rows(a["ln_ffn_b_2"])),
            ("b_mod", by_rows(a["b_mod_2"])), ("b_dw_f", by_rows(a["b_dw_f"])),
            ("w_dw_a", a["w_dw_a"].rearrange("l t (n p) -> (l t n) p", p=P)),
            ("w_dw_f", a["w_dw_f"].rearrange("l t (n p) -> (l t n) p", p=P)),
        ]
        row_of, rows = {}, 0
        for name, v in vectors:
            row_of[name] = rows
            rows += v.shape[0]
        VT = -(-rows // P)
        cols = sb("cols", [P, VT * P])

        with ExitStack() as side:
            hH = sb("hH", [P, KD, SEQ], F32R, side)
            hL = sb("hL", [P, KD, SEQ], F32R, side)
        with ExitStack() as side:
            qS = sb("qS", [P, 2, SEQ], F32, side)
            kS = sb("kS", [P, 2, SEQ], F32, side)
            with ExitStack() as early:
                mod_ring = sb("mod_ring", [P, MOD_SLOTS, MOD_STRIP], F32, early)
            gate_rows = sb("gate_rows", [P, FOX, SEQ], F32, side)
        with ExitStack() as side:
            stickQ = sb("stickQ", [P, SEQ], F32, side)
            stickK = sb("stickK", [P, SEQ], F32, side)
            keep = sb("keep", [P, 2, 1280], F32, side)
            stick_w = sb("stick_w", [P, 2, 1280], F32, side)
        sb("side", [P, 2 * KD * SEQ])
        with ExitStack() as main:
            tok_x = sb("tok_x", [P, QT, D], F32, main)
            tok_mem = sb("tok_mem", [P, 2, D], F32, main)
            memT = sb("memT", [P, KD, MEM], F32, main)
            vec_rows = sb("vec_rows", [P, VT, P], F32, main)
            pos_int = sb("pos_int", [P, SEQ], I32, main)
            angle = sb("angle", [P, 4, SEQ], F32, main)
        with ExitStack() as main:
            gH = sb("gH", [P, HALF, SEQ], F32R, main)
            gL = sb("gL", [P, HALF, SEQ], F32R, main)
            ff_tmp = sb("ff_tmp", [P, 2, SEQ], F32, main)
        with ExitStack() as main:
            v_pad = sb("v_pad", [P, NCONV, SEQ + TAPS - 1], F32, main)
            y = sb("y", [P, NCONV, SEQ], F32, main)
            q_mem0 = sb("q_mem0", [P, 2, SEQ], F32, main)
            mod_rows = sb("mod_rows", [P, 8, SEQ], F32, main)
        with ExitStack() as main:
            foxQ = sb("foxQ", [P, 6, SEQ], F32, main)
            foxK = sb("foxK", [P, 6, SEQ], F32, main)
            foxV = sb("foxV", [P, QT, CONV], F32, main)
            q_mem1 = sb("q_mem1", [P, 2, SEQ], F32, main)
            with ExitStack() as before_heads:
                gate = sb("gate", [P, SEQ], F32, before_heads)
                pick = sb("pick", [P, FOX, P], F32, before_heads)
            gateS = sb("gateS", [P, 4, SEQ], F32, main)
        with ExitStack() as main:
            stQ = sb("stQ", [P, 4, SEQ], F32, main)
            stK = sb("stK", [P, 4, SEQ], F32, main)
            stV = sb("stV", [P, QT, 512], F32, main)
            spQ = sb("spQ", [P, 4, SEQ], F32, main)
            spK = sb("spK", [P, 2, SEQ], F32, main)
            ixQ = sb("ixQ", [P, 2, SEQ], F32, main)
            spV = sb("spV", [P, QT, P], F32, main)
            chosen = sb("chosen", [P, QT, SEQ], F32, main)
        with ExitStack() as main:
            difQ = sb("difQ", [P, 8, SEQ], F32, main)
            difK = sb("difK", [P, 8, SEQ], F32, main)
            difV = sb("difV", [P, QT, D], F32, main)
        with ExitStack() as main:
            tok_out = sb("tok_out", [P, QT, D], F32, main)
        ps = ctx.enter_context(nc.psum_tensor("ps", [P, 8, SEQ], F32))

        def col(name, k):
            k = k + row_of[name]
            return cols[:, k:k + 1] if isinstance(k, int) else cols[:, bass.ds(k, 1)]

        def one_col(t, k):
            return t[:, k:k + 1] if isinstance(k, int) else t[:, bass.ds(k, 1)]

        def at(t, k, lo=0, hi=SEQ):
            return t[:, k, lo:hi] if isinstance(k, int) else t[:, bass.ds(k, 1), lo:hi].rearrange("p a n -> p (a n)")

        def span(t, lo, n):
            return t[:, :, lo:lo + n] if isinstance(lo, int) else t[:, :, bass.ds(lo, n)]

        class Signal:
            made = []

            def __init__(self, name, engine):
                self.sem = ctx.enter_context(nc.semaphore(name))
                self.count = START
                self.engine = engine
                Signal.made.append(self)

            def reserve(self, n):
                first = self.count
                self.count += n
                return first

        def sem(name):
            return ctx.enter_context(nc.semaphore(name))
        tensor_done, scalar_done, vector_done = sem("tensor_done"), sem("scalar_done"), sem("vector_done")
        constants_in, vectors_in, tokens_in, tables_in = sem("constants_in"), sem("vectors_in"), sem("tokens_in"), sem("tables_in")
        raw_landed = [sem("raw_landed0"), sem("raw_landed1")]
        raw_free = [sem("raw_free0"), sem("raw_free1")]
        mod_landed = [sem("mod_landed%d" % u) for u in range(MOD_SLOTS)]
        mod_free = [sem("mod_free%d" % u) for u in range(MOD_SLOTS)]
        out_written = sem("out_written")
        turn = {}
        strip_split = Signal("strip_split", "pool")
        tile_done = Signal("tile_done", "pe")
        summed, sums_in, turned_heads = Signal("summed", "pe"), Signal("sums_in", "pe"), Signal("turned_heads", "pe")
        logits_in, turned_in, value_in = Signal("logits_in", "pe"), Signal("turned_in", "pe"), Signal("value_in", "pe")
        stick_z, stick_sum, stick_pv = Signal("stick_z", "pe"), Signal("stick_sum", "pe"), Signal("stick_pv", "pe")
        index_in = Signal("index_in", "pe")
        mod_formed = Signal("mod_formed", "pe")
        mod_taken = Signal("mod_taken", "act")
        taken_act = Signal("taken_act", "act")
        squares, roots, highs = Signal("squares", "act"), Signal("roots", "act"), Signal("highs", "act")
        swapped, gates = Signal("swapped", "act"), Signal("gates", "act")
        ff_pre, ff_silu, ff_high = Signal("ff_pre", "act"), Signal("ff_silu", "act"), Signal("ff_high", "act")
        staged, exp_in, turned_act = Signal("staged", "act"), Signal("exp_in", "act"), Signal("turned_act", "act")
        stick_log, stick_wt, relus = Signal("stick_log", "act"), Signal("stick_wt", "act"), Signal("relus", "act")
        taken_dve = Signal("taken_dve", "dve")
        residual_in = Signal("residual_in", "dve")
        parts, lows, centred = Signal("parts", "dve"), Signal("lows", "dve"), Signal("centred", "dve")
        ff_conv, ff_prod, ff_low = Signal("ff_conv", "dve"), Signal("ff_prod", "dve"), Signal("ff_low", "dve")
        max_in, turned_dve, head_out = Signal("max_in", "dve"), Signal("turned_dve", "dve"), Signal("head_out", "dve")
        stick_keep, stick_out, scored = Signal("stick_keep", "dve"), Signal("stick_out", "dve"), Signal("scored", "dve")

        def start_signals(eng, name):
            for s in Signal.made:
                if s.engine == name:
                    eng.sem_inc(s.sem, START)

        def alone(eng, i):
            if not isinstance(i, int):
                eng.sem_inc(turn[id(eng)], 1)

        def turns(eng, n, first=0):
            if n - first > 1:
                with eng.Fori(first, n) as i:
                    yield i
            elif n - first == 1:
                yield first

        def strips(eng, n, first=0):
            for i in turns(eng, n // 2, first):
                yield i * 2, 0, i
                yield i * 2 + 1, 1, i
            if n % 2 and n // 2 >= first:
                yield n - 1, 0, n // 2

        class Run:
            raws = splits = 0
            landed = [0, 0]

            def __init__(self, form, count, kt, pieces, take, width=STRIP, tokens=SEQ):
                self.form, self.count, self.kt, self.pieces, self.take = form, count, kt, pieces, take
                self.width, self.npieces, self.tokens = width, len(pieces(0)), tokens
                self.r0, self.n0 = Run.raws, Run.splits
                self.landed0 = [Run.landed[(self.r0 + u) % 2] for u in range(2)]
                Run.raws += count
                for s in range(count):
                    Run.landed[(self.r0 + s) % 2] += 16 * self.npieces
                Run.splits += count
                self.tile0 = tile_done.reserve(2 * count)
                self.split0 = strip_split.reserve(count)
                self.act0, self.dve0 = taken_act.count, taken_dve.count
                if take.by_act:
                    taken_act.reserve(count)
                if take.by_dve:
                    taken_dve.reserve(count)
                take.attach(self)
                runs.append(self)

            def raw_slot(self, u):
                return (self.r0 + u) % 2

            def part_slot(self, u):
                return (self.n0 + u) % 2

            def bank(self, u, f):
                return 2 * self.part_slot(u) + f

            def wait_landed(self, eng, u, i):
                size = 16 * self.npieces
                eng.wait_ge(raw_landed[self.raw_slot(u)], i * size + (self.landed0[u] + size))
                alone(eng, i)

            def load(self, sp):
                for s, u, i in strips(sp, self.count):
                    slot = self.raw_slot(u)
                    to = raw[:, slot, 0:self.kt * self.width].rearrange("p (k c) -> p k c", k=self.kt)
                    pieces = self.pieces(s)
                    sp.wait_ge(raw_free[slot], i + ((self.r0 + u) // 2 + 1))
                    alone(sp, i)
                    for lo, hi, src in pieces:
                        sp.dma_start(to[:, :, lo:hi], src).then_inc(raw_landed[slot], 16)

            def split(self, pool):
                n = self.kt * self.width
                for s, u, i in strips(pool, self.count):
                    slot, part = self.raw_slot(u), self.part_slot(u)
                    self.wait_landed(pool, u, i)
                    pool.wait_ge(tile_done.sem, s * 2 + (self.tile0 - 2))
                    alone(pool, s)
                    pool.tensor_tensor(wH[:, part, 0:n], raw[:, slot, 0:n], ones[:, 0:1].to_broadcast([P, n]), ALU.mult)
                    pool.drain()
                    pool.tensor_tensor(wL[:, part, 0:n], raw[:, slot, 0:n], wH[:, part, 0:n].bitcast(F32),
                                       ALU.subtract).then_inc(strip_split.sem, 1)
                    pool.drain().then_inc(raw_free[slot], 1)

            def multiply_strip(self, pe, s, u, srcH, srcL, gate=None):
                part, w = self.part_slot(u), self.width
                pe.wait_ge(strip_split.sem, s + (self.split0 + 1))
                alone(pe, s)
                pe.wait_ge(taken_act.sem, s + (self.act0 - 1) if self.take.by_act else self.act0)
                alone(pe, s)
                pe.wait_ge(taken_dve.sem, s + (self.dve0 - 1) if self.take.by_dve else self.dve0)
                alone(pe, s)
                products = [(wH, srcH, "high"), (wL, srcH, None), (wH, srcL, "low")]

                def groups(f):
                    bank = self.bank(u, f)
                    if self.form == "A" and f * P < w:
                        yield ps[:, bank, 0:self.tokens], lambda wp, hp, k: (
                            wp[:, part, k * w + f * P:k * w + f * P + P], hp[:, k, 0:self.tokens])
                    elif self.form == "B":
                        for j in range(2):
                            lo = (2 * f + j) * P
                            if lo < self.tokens:
                                yield ps[:, bank, j * w:j * w + w], lambda wp, hp, k, lo=lo: (
                                    hp[:, k, lo:lo + P], wp[:, part, k * w:k * w + w])
                every, last_k = range(self.kt), self.kt - 1
                if gate:
                    order = [(f, ts, range(last_k)) for ts in ((0, 1), (2,)) for f in range(2)] + [(f, (0, 1, 2), [last_k]) for f in range(2)]
                else:
                    order = [(f, (0, 1, 2), every) for f in range(2)]
                for f, ts, ks in order:
                    last = None
                    for dst, operands in groups(f):
                        for t in ts:
                            wp, hp, which = products[t]
                            for k in ks:
                                if gate and f == 0:
                                    gate(pe, which, k)
                                left, right = operands(wp, hp, k)
                                last = pe.matmul(dst, left, right, start=(t == 0 and k == 0), stop=(t == 2 and k == last_k))
                    if last_k in ks:
                        (last or pe.drain()).then_inc(tile_done.sem, 1)

            def multiply(self, pe, srcH, srcL, gate=None):
                if gate:
                    for u in range(min(2, self.count)):
                        self.multiply_strip(pe, u, u, srcH, srcL, gate if u == 0 else None)
                for s, u, i in strips(pe, self.count, 1 if gate else 0):
                    if not (gate and self.count == 1):
                        self.multiply_strip(pe, s, u, srcH, srcL)

            def wait_tile(self, eng, s, f):
                eng.wait_ge(tile_done.sem, s * 2 + (self.tile0 + f + 1))
                alone(eng, s)

        runs = []

        def columns(w, lo, n, k0=0, kt=KD):
            return span(w.rearrange("(k p) c -> p k c", p=P)[:, k0:k0 + kt, :], lo, n)

        def plain(w, lo=0, k0=0, kt=KD):
            return lambda s: [(0, STRIP, columns(w, s * STRIP + lo, STRIP, k0, kt))]

        def pairs_of(w1, lo1, w2, lo2):
            return lambda s: [(0, P, columns(w1, s * P + lo1, P)), (P, STRIP, columns(w2, s * P + lo2, P))]

        class Take:
            by_act = by_dve = True

            def attach(self, run):
                self.run = run

            def scalar(self, act):
                pass

        class TakeCopy(Take):
            def __init__(self, dst, n=SEQ, first=0):
                self.dst, self.n, self.first = dst, n, first

            def scalar(self, act):
                r = self.run
                for s, u, i in strips(act, r.count):
                    r.wait_tile(act, s, 0)
                    act.activation(at(self.dst, s * 2 + self.first, 0, self.n), ps[:, r.bank(u, 0), 0:self.n],
                                   ACT.Copy).then_inc(taken_act.sem, 1)

            def vector(self, dve):
                r = self.run
                for s, u, i in strips(dve, r.count):
                    r.wait_tile(dve, s, 1)
                    dve.tensor_copy(at(self.dst, s * 2 + (self.first + 1), 0, self.n), ps[:, r.bank(u, 1), 0:self.n]
                                    ).then_inc(taken_dve.sem, 1)

        class TakeValues(Take):
            def __init__(self, dst):
                self.dst = dst

            def bank(self, u, f):
                r = self.run
                return ps[:, r.bank(u, f), 0:2 * r.width].rearrange("p (t c) -> p t c", t=2)

            def scalar(self, act):
                r = self.run
                for s, u, i in strips(act, r.count):
                    r.wait_tile(act, s, 0)
                    act.activation(span(self.dst[:, 0:2, :], s * r.width, r.width), self.bank(u, 0), ACT.Copy
                                   ).then_inc(taken_act.sem, 1)

            def vector(self, dve):
                r = self.run
                for s, u, i in strips(dve, r.count):
                    r.wait_tile(dve, s, 1)
                    dve.tensor_copy(span(self.dst[:, 2:4, :], s * r.width, r.width), self.bank(u, 1)
                                    ).then_inc(taken_dve.sem, 1)

        class TakeMemV(Take):
            def __init__(self, layer):
                self.layer = layer

            def scalar(self, act):
                self.run.wait_tile(act, 0, 0)
                act.activation(memV[:, 2 * self.layer, :], ps[:, self.run.bank(0, 0), 0:MEM], ACT.Copy).then_inc(taken_act.sem, 1)

            def vector(self, dve):
                self.run.wait_tile(dve, 0, 1)
                dve.wait_ge(taken_act.sem, self.run.act0 + 1)
                dve.tensor_copy(memV[:, 2 * self.layer + 1, :], ps[:, self.run.bank(0, 0), MEM:2 * MEM]).then_inc(taken_dve.sem, 1)

        class TakeRope(Take):
            by_act = False

            def __init__(self, dst):
                self.dst = dst

            def attach(self, run):
                self.run = run
                self.swap0 = swapped.reserve(2 * run.count)

            def scalar(self, act):
                r = self.run
                for s, u, i in strips(act, r.count):
                    act.wait_ge(taken_dve.sem, s + (r.dve0 - 1))
                    alone(act, s)
                    for f in range(2):
                        r.wait_tile(act, s, f)
                        for q in range(4):
                            o = 32 * (q ^ 1)
                            last = act.activation(tmpA[o:o + 32, r.bank(u, f), :], ps[32 * q:32 * q + 32, r.bank(u, f), :], ACT.Copy)
                        last.then_inc(swapped.sem, 1)

            def vector(self, dve):
                r = self.run
                for s, u, i in strips(dve, r.count):
                    for f in range(2):
                        dve.wait_ge(swapped.sem, s * 2 + (self.swap0 + f + 1))
                        alone(dve, s)
                        k = r.bank(u, f)
                        dve.tensor_tensor(tmpB[:, k, :], ps[:, r.bank(u, f), :], cosT[:, :], ALU.mult)
                        dve.tensor_tensor(tmpA[:, k, :], tmpA[:, k, :], sinT[:, :], ALU.mult)
                        dve.drain()
                        dve.tensor_tensor(at(self.dst, s * 2 + f), tmpB[:, k, :], tmpA[:, k, :], ALU.add)
                    dve.drain().then_inc(taken_dve.sem, 1)

        class TakeResidual(Take):
            by_act = False

            def __init__(self, gain=None, then=None):
                self.gain, self.then = gain, then

            def attach(self, run):
                self.run = run
                if self.then == "square":
                    self.in0, self.square0 = residual_in.reserve(2 * run.count), squares.reserve(2 * run.count)

            def scalar(self, act):
                r = self.run
                if self.then:
                    fetch_root(act)
                if self.then == "square":
                    for s, u, i in strips(act, r.count):
                        for f in range(2):
                            act.wait_ge(residual_in.sem, s * 2 + (self.in0 + f + 1))
                            alone(act, s)
                            act.activation(tmpA[:, r.bank(u, f), :], at(xT, s * 2 + f), ACT.Square).then_inc(squares.sem, 1)

            def vector(self, dve):
                r = self.run
                if self.then:
                    dve.memset(acc[:, :], 0.0)
                for s, u, i in strips(dve, r.count):
                    for f in range(2):
                        r.wait_tile(dve, s, f)
                        t, x = ps[:, r.bank(u, f), :], at(xT, s * 2 + f)
                        if self.gain is None:
                            last = dve.tensor_tensor(x, t, x, ALU.add)
                        else:
                            last = dve.scalar_tensor_tensor(x, t, one_col(mod_plus, s * 2 + (self.gain + f)), x, ALU.mult, ALU.add)
                        if self.then == "square":
                            last.then_inc(residual_in.sem, 1)
                            dve.wait_ge(squares.sem, s * 2 + (self.square0 + f + 1))
                            alone(dve, s)
                            last = dve.tensor_tensor(acc[:, :], acc[:, :], tmpA[:, r.bank(u, f), :], ALU.add)
                        elif self.then == "sum":
                            dve.drain()
                            last = dve.tensor_tensor(acc[:, :], acc[:, :], x, ALU.add)
                        if f == 0 and self.then:
                            dve.drain()
                    if self.then:
                        dve.drain().then_inc(taken_dve.sem, 1)
                    else:
                        last.then_inc(taken_dve.sem, 1)

        class TakeGlu(Take):
            by_act = False

            def attach(self, run):
                self.run = run
                self.gate0 = gates.reserve(run.count)

            def scalar(self, act):
                r = self.run
                for s, u, i in strips(act, r.count):
                    r.wait_tile(act, s, 1)
                    act.wait_ge(taken_dve.sem, s + (r.dve0 - 1))
                    alone(act, s)
                    act.activation(tmpA[:, u, :], ps[:, r.bank(u, 1), :], ACT.Sigmoid, bias=col("b_glu", s + NCONV)
                                   ).then_inc(gates.sem, 1)

            def vector(self, dve):
                r = self.run
                for s, u, i in strips(dve, r.count):
                    dve.wait_ge(gates.sem, s + (self.gate0 + 1))
                    alone(dve, s)
                    dve.scalar_tensor_tensor(at(v_pad, s, TAPS - 1, TAPS - 1 + SEQ), ps[:, r.bank(u, 0), :], col("b_glu", s),
                                             tmpA[:, u, :], ALU.add, ALU.mult).then_inc(taken_dve.sem, 1)

        class TakeForget(Take):
            by_dve = False

            def scalar(self, act):
                self.run.wait_tile(act, 0, 0)
                act.activation(gate[0:FOX, :], ps[0:FOX, self.run.bank(0, 0), :], ACT.Identity, bias=gate_bias[0:FOX, :]
                               ).then_inc(taken_act.sem, 1)

            def vector(self, dve):
                pass

        class TakeFF(Take):
            by_act = False

            def __init__(self, half, conv=None):
                self.half, self.conv = half, conv

            def attach(self, run):
                self.run = run
                n = run.count
                self.pre0 = ff_pre.reserve(n) if self.conv is not None else 0
                self.conv0 = ff_conv.reserve(n) if self.conv is not None else 0
                self.silu0, self.high0 = ff_silu.reserve(n), ff_high.reserve(n)
                self.prod0, self.low0 = ff_prod.reserve(n), ff_low.reserve(n)

            def weight(self, tap, s, f):
                k = tap * 2 * FT + f * FT + self.half * HALF
                return col("w_dw_f", s + (self.conv * 3 * 2 * FT + k))

            def scalar(self, act):
                r = self.run
                for s, u, i in strips(act, r.count):
                    if self.conv is not None:
                        act.wait_ge(ff_prod.sem, s + (self.prod0 - 1))
                        alone(act, s)
                        for f in range(2):
                            r.wait_tile(act, s, f)
                            bias = col("b_dw_f", s + (self.conv * 2 * FT + f * FT + self.half * HALF))
                            last = act.activation(tmpA[:, 2 * u + f, :], ps[:, r.bank(u, f), :], ACT.Identity, bias=bias,
                                                  scale=self.weight(2, s, f))
                        last.then_inc(ff_pre.sem, 1)
                        act.wait_ge(ff_conv.sem, s + (self.conv0 + 1))
                        alone(act, s)
                        gate_in = tmpA[:, 2 * u, :]
                    else:
                        act.wait_ge(ff_prod.sem, s + (self.prod0 - 1))
                        alone(act, s)
                        r.wait_tile(act, s, 0)
                        gate_in = ps[:, r.bank(u, 0), :]
                    act.activation(tmpB[:, u, :], gate_in, ACT.Silu).then_inc(ff_silu.sem, 1)
                    act.wait_ge(ff_prod.sem, s + (self.prod0 + 1))
                    alone(act, s)
                    act.activation(at(gH, s), ff_tmp[:, u, :], ACT.Copy).then_inc(ff_high.sem, 1)

            def vector(self, dve):
                r = self.run
                for s, u, i in strips(dve, r.count):
                    if self.conv is not None:
                        dve.wait_ge(ff_pre.sem, s + (self.pre0 + 1))
                        alone(dve, s)
                        for back in (1, 2):
                            for f in range(2):
                                t = tmpA[:, 2 * u + f, back:SEQ]
                                last = dve.scalar_tensor_tensor(t, ps[:, r.bank(u, f), 0:SEQ - back], self.weight(2 - back, s, f),
                                                                t, ALU.mult, ALU.add)
                            dve.drain()
                        dve.drain().then_inc(ff_conv.sem, 1)
                        value = tmpA[:, 2 * u + 1, :]
                    else:
                        r.wait_tile(dve, s, 1)
                        value = ps[:, r.bank(u, 1), :]
                    dve.wait_ge(ff_silu.sem, s + (self.silu0 + 1))
                    alone(dve, s)
                    dve.tensor_tensor(ff_tmp[:, u, :], value, tmpB[:, u, :], ALU.mult).then_inc(ff_prod.sem, 1)
                    dve.drain().then_inc(taken_dve.sem, 1)
                    dve.wait_ge(ff_high.sem, s + (self.high0 + 1))
                    alone(dve, s)
                    dve.tensor_tensor(at(gL, s), ff_tmp[:, u, :], at(gH, s).bitcast(F32), ALU.subtract).then_inc(ff_low.sem, 1)

            def gate(self, pe, which, k):
                if which == "high":
                    pe.wait_ge(ff_high.sem, self.high0 + k + 1)
                elif which == "low":
                    pe.wait_ge(ff_low.sem, self.low0 + k + 1)

        class Parts:
            tiles = range(KD)

            def reserve(self):
                self.high0, self.low0 = highs.reserve(len(self.tiles)), lows.reserve(len(self.tiles))

            def gate(self, pe, which, k):
                if k in self.tiles:
                    n = k - self.tiles[0] + 1
                    if which == "high":
                        pe.wait_ge(highs.sem, self.high0 + n)
                    elif which == "low":
                        pe.wait_ge(lows.sem, self.low0 + n)

            def tensor(self, pe):
                pass

            def scalar(self, act):
                for k in range(KD):
                    act.wait_ge(parts.sem, self.part0 + k + 1)
                    act.activation(hH[:, k, 0:self.n], whole(k, self.n), ACT.Copy).then_inc(highs.sem, 1)

            def lows(self, dve):
                for k in range(KD):
                    dve.wait_ge(highs.sem, self.high0 + k + 1)
                    dve.tensor_tensor(hL[:, k, 0:self.n], whole(k, self.n), hH[:, k, 0:self.n].bitcast(F32),
                                      ALU.subtract).then_inc(lows.sem, 1)

        def whole(k, n=SEQ):
            return (tmpA if k < 4 else tmpB)[:, k % 4, 0:n]

        def square_sum(pe, weight, square0, bank, tiles, n):
            for k in range(tiles):
                pe.wait_ge(squares.sem, square0 + k + 1)
                pe.matmul(ps[:, bank, 0:n], weight[:, :], tmpA[:, k % 4, 0:n], start=(k == 0), stop=(k == tiles - 1)
                          ).then_inc(summed.sem, 1)

        def fetch_root(act):
            act.activation(spare, eps_ln, ACT.Sqrt)

        def square_tiles(act, src, square0, summed0, tiles, n, centred0=None):
            fetch_root(act)
            for k in range(tiles):
                if centred0 is not None:
                    act.wait_ge(centred.sem, centred0 + k + 1)
                act.wait_ge(summed.sem, summed0 + k - 3)
                act.activation(tmpA[:, k % 4, 0:n], src[:, k, 0:n], ACT.Square).then_inc(squares.sem, 1)

        class RmsParts(Parts):
            def __init__(self, src, name, g0=0, n=SEQ, stats="own"):
                self.src, self.name, self.g0, self.n, self.stats = src, name, g0, n, stats
                if stats == "own":
                    self.square0 = squares.reserve(KD)
                self.tiles_summed = {"own": KD, "acc": 1, "none": 0}[stats]
                self.summed0 = summed.reserve(self.tiles_summed)
                self.root0 = roots.reserve(1) if self.tiles_summed else 0
                self.part0 = parts.reserve(KD)
                self.reserve()

            def tensor(self, pe):
                if self.stats == "own":
                    square_sum(pe, mean_of, self.square0, 7, KD, self.n)
                elif self.stats == "acc":
                    pe.matmul(ps[:, 7, :], mean_of[:, :], acc[:, :], start=True, stop=True).then_inc(summed.sem, 1)

            def scalar(self, act):
                if self.stats == "own":
                    square_tiles(act, self.src, self.square0, self.summed0, KD, self.n)
                if self.stats != "none":
                    act.wait_ge(summed.sem, self.summed0 + self.tiles_summed)
                    act.activation(rstd[:, 0:self.n], ps[:, 7, 0:self.n], ACT.Sqrt, bias=eps_rms).then_inc(roots.sem, 1)
                Parts.scalar(self, act)

            def vector(self, dve):
                if self.stats != "none":
                    dve.wait_ge(roots.sem, self.root0 + 1)
                    dve.reciprocal(rstd[:, 0:self.n], rstd[:, 0:self.n])
                    dve.drain()
                for k in range(KD):
                    dve.scalar_tensor_tensor(whole(k, self.n), self.src[:, k, 0:self.n], col(self.name, self.g0 + k),
                                             rstd[:, 0:self.n], ALU.mult, ALU.mult).then_inc(parts.sem, 1)
                self.lows(dve)

        class ModParts(Parts):
            n = SEQ

            def __init__(self, layer, shift, scale):
                self.shift, self.scale = 48 * layer + KD * shift, 48 * layer + KD * scale
                self.part0 = parts.reserve(KD)
                self.reserve()

            def scalar(self, act):
                Parts.scalar(self, act)
                for k in range(KD):
                    act.activation(xT[:, k, :], xT[:, k, :], ACT.Copy, scale=ALPHA)

            def vector(self, dve):
                for k in range(KD):
                    dve.tensor_scalar(whole(k), xT[:, k, :], mod_plus[:, self.scale + k:self.scale + k + 1],
                                      mod[:, self.shift + k:self.shift + k + 1], ALU.mult, ALU.add).then_inc(parts.sem, 1)
                self.lows(dve)

        class HeadParts(Parts):
            def __init__(self, sources, first=0, gain=None, factor=1.0):
                self.sources, self.gain, self.factor = sources, gain, factor
                self.tiles = range(first, first + len(sources))
                self.turn0 = turned_heads.reserve(len(sources))
                self.reserve()

            def tensor(self, pe):
                for n, (src, t) in enumerate(self.sources):
                    pe.wait_ge(lows.sem, self.low0 + n - 3)
                    for q in range(QT):
                        last = pe.transpose(ps[:, 4 + n % 4, q * P:q * P + P], src[:, t, q * P:q * P + P], ident[:, :])
                    last.then_inc(turned_heads.sem, 1)

            def scalar(self, act):
                for n, k in enumerate(self.tiles):
                    act.wait_ge(turned_heads.sem, self.turn0 + n + 1)
                    act.activation(hH[:, k, :], ps[:, 4 + n % 4, :], ACT.Copy,
                                   scale=1.0 if self.gain is None else self.gain).then_inc(highs.sem, 1)

            def vector(self, dve):
                for n, k in enumerate(self.tiles):
                    dve.wait_ge(highs.sem, self.high0 + n + 1)
                    dve.scalar_tensor_tensor(hL[:, k, :], ps[:, 4 + n % 4, :], 1.0 if self.gain is None else self.gain,
                                             hH[:, k, :].bitcast(F32), ALU.mult, ALU.subtract).then_inc(lows.sem, 1)

        stages = []

        class Stage:
            def __init__(self):
                stages.append(self)

            def tensor(self, pe):
                pass

            def scalar(self, act):
                pass

            def vector(self, dve):
                pass

        class Products(Stage):
            def __init__(self, prepare, *made):
                super().__init__()
                self.prepare, self.runs = prepare, made

            def tensor(self, pe):
                self.prepare.tensor(pe)
                for n, run in enumerate(self.runs):
                    run.multiply(pe, hH, hL, self.prepare.gate if n == 0 else None)

            def scalar(self, act):
                self.prepare.scalar(act)
                for run in self.runs:
                    run.take.scalar(act)

            def vector(self, dve):
                self.prepare.vector(dve)
                for run in self.runs:
                    run.take.vector(dve)

        class FeedForward(Stage):
            def __init__(self, prepare, up, down, then, gain=None, conv=None):
                super().__init__()
                self.prepare = prepare
                self.halves = []
                for h in range(2):
                    go_up = Run("A", HALF, KD, up(h), TakeFF(h, conv))
                    go_down = Run("A", D // STRIP, HALF, plain(down, 0, h * HALF, HALF), TakeResidual(gain, then if h else None))
                    self.halves.append((go_up, go_down))

            def tensor(self, pe):
                self.prepare.tensor(pe)
                for h, (up, down) in enumerate(self.halves):
                    up.multiply(pe, hH, hL, self.prepare.gate if h == 0 else None)
                    down.multiply(pe, gH, gL, up.take.gate)

            def scalar(self, act):
                self.prepare.scalar(act)
                for up, down in self.halves:
                    up.take.scalar(act)
                    down.take.scalar(act)

            def vector(self, dve):
                self.prepare.vector(dve)
                for up, down in self.halves:
                    up.take.vector(dve)
                    down.take.vector(dve)

        class Constants(Stage):
            def tensor(self, pe):
                pe.wait_ge(constants_in, 1)
                pe.wait_ge(tokens_in, 32)
                n = 0
                for src, tiles in ((tok_mem, 2), (tok_x, QT)):
                    for k in range(KD):
                        pe.wait_ge(highs.sem, self.high0 + n - 3)
                        for t in range(tiles):
                            last = pe.transpose(ps[:, 4 + n % 4, t * P:t * P + P], src[:, t, k * P:k * P + P], ident[:, :])
                        last.then_inc(turned_heads.sem, 1)
                        n += 1
                pe.wait_ge(vectors_in, 16 * len(vector_loads))
                for j in range(VT):
                    pe.transpose(ps[:, j // 4, (j % 4) * P:(j % 4) * P + P], vec_rows[:, j, :], ident[:, :])

            def __init__(self):
                super().__init__()
                self.turn0, self.high0 = turned_heads.reserve(2 * KD), highs.reserve(2 * KD)

            def scalar(self, act):
                n = 0
                for dst, w in ((memT, MEM), (xT, SEQ)):
                    for k in range(KD):
                        act.wait_ge(turned_heads.sem, self.turn0 + n + 1)
                        act.activation(dst[:, k, 0:w], ps[:, 4 + n % 4, 0:w], ACT.Copy).then_inc(highs.sem, 1)
                        n += 1

            def vector(self, dve):
                dve.wait_ge(constants_in, 1)
                dve.tensor_copy(identR[:, :], ident[:, :])
                dve.tensor_copy(causalR[:, :], causal[:, :])
                dve.tensor_copy(beforeR[:, :], before[:, :])
                dve.memset(eps_rms, RMS_EPS)
                dve.memset(eps_ln, LN_EPS)
                dve.wait_ge(tables_in, 16 * 7)
                dve.tensor_copy(angle[:, 0, :], pos_int[:, :])
                dve.drain()
                dve.tensor_scalar(angle[:, 0, :], angle[:, 0, :], rope_inv, None, ALU.mult)
                dve.drain()
                for n, quarter in ((1, 0.0), (2, 0.25)):
                    dve.tensor_scalar(angle[:, 3, :], angle[:, 0, :], 1.0 / (2.0 * math.pi), quarter, ALU.mult, ALU.add)
                    dve.drain()
                    dve.tensor_scalar(angle[:, 3, :], angle[:, 3, :], ROUND, None, ALU.add)
                    dve.drain()
                    dve.tensor_scalar(angle[:, 3, :], angle[:, 3, :], ROUND, None, ALU.subtract)
                    dve.drain()
                    dve.scalar_tensor_tensor(angle[:, n, :], angle[:, 3, :], -TWO_PI_HIGH, angle[:, 0, :], ALU.mult, ALU.add)
                    dve.drain()
                    dve.scalar_tensor_tensor(angle[:, n, :], angle[:, 3, :], -TWO_PI_LOW, angle[:, n, :], ALU.mult, ALU.add)
                    dve.drain()
                    dve.tensor_scalar(angle[:, n, :], angle[:, n, :], quarter * 2.0 * math.pi, math.pi * (1 - 2.0 ** -22), ALU.add, ALU.min)
                    dve.drain()
                    dve.tensor_scalar(angle[:, n, :], angle[:, n, :], -math.pi * (1 - 2.0 ** -22), None, ALU.max)
                    dve.drain()
                for n in range(2):
                    dve.tensor_tensor_reduce(out=tmpA[:, n, 0:DH], in0=lams[:, 2 * n, :], in1=lams[:, 2 * n + 1, :], scale=1.0,
                                             scalar=0.0, op0=ALU.mult, op1=ALU.add, accum_out=dots[:, n:n + 1])

        class Tables(Stage):
            def scalar(self, act):
                for j in range(0, VT, 4):
                    w = min(4, VT - j) * P
                    act.activation(cols[:, j * P:j * P + w], ps[:, j // 4, 0:w], ACT.Copy)
                act.drain()
                act.activation(silu_c[:, :, 0], cols[:, row_of["c"]:row_of["c"] + KD], ACT.Silu)
                act.activation(sinT[:, :], angle[:, 1, :], ACT.Sin)
                act.activation(cosT[:, :], angle[:, 2, :], ACT.Sin)
                act.activation(dot_exp, dots, ACT.Exp)

        class Lambda(Stage):
            def vector(self, dve):
                dve.tensor_scalar(sinT[:, :], sinT[:, :], rope_sign, None, ALU.mult)
                dve.tensor_tensor(neg_lam, dot_exp[:, 1:2], dot_exp[:, 0:1], ALU.subtract)
                dve.drain()
                dve.tensor_scalar(neg_lam, neg_lam, LAMBDA_INIT, None, ALU.subtract)
                dve.memset(v_pad[:, :, 0:TAPS - 1], 0.0)

        class Modulation:
            def __init__(self):
                self.after = len(stages)
                self.formed0, self.taken0 = mod_formed.reserve(8), mod_taken.reserve(8)
                runs.append(self)

            def load(self, sp):
                sp.wait_ge(tensor_done, self.after)
                for l in range(2):
                    for i in turns(sp, 4):
                        for k in range(KD):
                            u = k % MOD_SLOTS
                            sp.wait_ge(mod_free[u], i * 2 + (8 * l + k // MOD_SLOTS + 1))
                            alone(sp, i)
                            w_rows = a["w_mod_2"][l][k * P:k * P + P, :]
                            sp.dma_start(mod_ring[:, u, :], w_rows[:, bass.ds(i * MOD_STRIP, MOD_STRIP)]).then_inc(mod_landed[u], 16)

            def split(self, pool):
                pass

            def multiply(self, pe):
                for i in turns(pe, 4):
                    for bank in range(2):
                        pe.wait_ge(mod_taken.sem, i * 2 + (self.taken0 + bank - 1))
                        alone(pe, i)
                        for k in range(KD):
                            u = k % MOD_SLOTS
                            pe.wait_ge(mod_landed[u], i * 64 + 16 * (2 * bank + k // MOD_SLOTS + 1))
                            alone(pe, i)
                            for g in range(3):
                                last = pe.matmul(ps[GROUP * g:GROUP * g + GROUP, bank, :], silu_c[:, k, :], mod_ring[:, u, g * SEQ:g * SEQ + SEQ],
                                                 start=(k == 0), stop=(k == KD - 1))
                            last.then_inc(mod_free[u], 1)
                        pe.drain().then_inc(mod_formed.sem, 1)

            def take(self, act):
                for i in turns(act, 4):
                    for bank in range(2):
                        act.wait_ge(mod_formed.sem, i * 2 + (self.formed0 + bank + 1))
                        alone(act, i)
                        act.activation(at(mod_rows[0:3 * GROUP], i * 2 + bank), ps[0:3 * GROUP, bank, :], ACT.Copy).then_inc(mod_taken.sem, 1)

        class Conv(Stage):
            def __init__(self, modulation):
                super().__init__()
                self.modulation = modulation

            def tensor(self, pe):
                self.modulation.multiply(pe)

            def scalar(self, act):
                self.modulation.take(act)

            def vector(self, dve):
                for j in range(NCONV):
                    dve.tensor_scalar(y[:, j, :], v_pad[:, j, 0:SEQ], col("w_dw_a", j), col("b_dw_a", j), ALU.mult, ALU.add)
                dve.drain()
                for i in turns(dve, (TAPS - 1) // 5):
                    for u in range(5):
                        for j in range(NCONV):
                            dve.scalar_tensor_tensor(y[:, j, :], v_pad[:, j, bass.ds(i * 5 + (u + 1), SEQ)],
                                                     col("w_dw_a", i * (5 * NCONV) + ((u + 1) * NCONV + j)), y[:, j, :], ALU.mult, ALU.add)
                        dve.drain()

        class ModTurn(Stage):
            def tensor(self, pe):
                w = 3 * GROUP
                for b in range(32):
                    pe.transpose(ps[:, b // 4, b % 4 * w:b % 4 * w + w], mod_rows[0:w, b // 4, b % 4 * P:b % 4 * P + P], ident[0:w, 0:w])

        class ModBias(Stage):
            def vector(self, dve):
                turned = ps[:, :, 0:12 * GROUP].rearrange("p j (c g q) -> p j c g q", c=4, q=GROUP)
                bias = cols[:, row_of["b_mod"]:row_of["b_mod"] + 96].rearrange("p (j g c) -> p j g c", j=8, g=3)
                to = mod[:, :].rearrange("p (j g c) -> p j g c", j=8, g=3)
                for g in range(3):
                    dve.tensor_tensor(to[:, :, g, :], turned[:, :, :, g, 0], bias[:, :, g, :], ALU.add)
                dve.drain()
                dve.tensor_scalar(mod_plus[:, :], mod[:, :], 1.0, None, ALU.add)

        class LayerNorm(Stage):
            def __init__(self, buf, tiles, gname, bname, k0=0, silu=False, summed_up=True):
                super().__init__()
                self.buf, self.tiles, self.gname, self.bname, self.k0, self.silu = buf, tiles, gname, bname, k0, silu
                self.summed_up = summed_up
                self.sum0, self.root0 = sums_in.reserve(1), roots.reserve(1)
                self.centred0, self.square0, self.summed0 = centred.reserve(tiles), squares.reserve(tiles), summed.reserve(tiles)
                self.part0 = parts.reserve(tiles)
                if silu:
                    self.high0, self.low0 = highs.reserve(tiles), lows.reserve(tiles)

            def tensor(self, pe):
                if self.summed_up:
                    last = pe.matmul(ps[:, 6, :], ones[:, :], acc[:, :], start=True, stop=True)
                else:
                    for k in range(self.tiles):
                        last = pe.matmul(ps[:, 6, :], ones[:, :], self.buf[:, k, :], start=(k == 0), stop=(k == self.tiles - 1))
                last.then_inc(sums_in.sem, 1)
                square_sum(pe, ones, self.square0, 7, self.tiles, SEQ)

            def scalar(self, act):
                square_tiles(act, self.buf, self.square0, self.summed0, self.tiles, SEQ, self.centred0)
                act.wait_ge(summed.sem, self.summed0 + self.tiles)
                act.activation(rstd[:, :], ps[:, 7, :], ACT.Sqrt, bias=eps_ln, scale=1.0 / (self.tiles * P)).then_inc(roots.sem, 1)
                for k in range(self.tiles):
                    act.wait_ge(parts.sem, self.part0 + k + 1)
                    if self.silu:
                        act.wait_ge(lows.sem, self.low0 + k - 3)
                        act.activation(tmpB[:, k % 4, :], self.buf[:, k, :], ACT.Silu, bias=col(self.bname, self.k0 + k))
                        act.drain()
                        act.activation(hH[:, k, :], tmpB[:, k % 4, :], ACT.Copy).then_inc(highs.sem, 1)
                    else:
                        act.activation(self.buf[:, k, :], self.buf[:, k, :], ACT.Identity, bias=col(self.bname, self.k0 + k))

            def vector(self, dve):
                width = 1.0 / (self.tiles * P)
                dve.wait_ge(sums_in.sem, self.sum0 + 1)
                for k in range(self.tiles):
                    dve.scalar_tensor_tensor(self.buf[:, k, :], ps[:, 6, :], -width, self.buf[:, k, :], ALU.mult, ALU.add).then_inc(centred.sem, 1)
                dve.wait_ge(roots.sem, self.root0 + 1)
                dve.reciprocal(rstd[:, :], rstd[:, :])
                dve.drain()
                for k in range(self.tiles):
                    dve.scalar_tensor_tensor(self.buf[:, k, :], self.buf[:, k, :], col(self.gname, self.k0 + k), rstd[:, :],
                                             ALU.mult, ALU.mult).then_inc(parts.sem, 1)
                if self.silu:
                    for k in range(self.tiles):
                        dve.wait_ge(highs.sem, self.high0 + k + 1)
                        dve.tensor_tensor(hL[:, k, :], tmpB[:, k % 4, :], hH[:, k, :].bitcast(F32), ALU.subtract).then_inc(lows.sem, 1)

        class FinalRms(Stage):
            def __init__(self):
                super().__init__()
                self.summed0, self.root0 = summed.reserve(1), roots.reserve(1)

            def tensor(self, pe):
                pe.matmul(ps[:, 7, :], mean_of[:, :], acc[:, :], start=True, stop=True).then_inc(summed.sem, 1)

            def scalar(self, act):
                act.wait_ge(summed.sem, self.summed0 + 1)
                act.activation(rstd[:, :], ps[:, 7, :], ACT.Sqrt, bias=eps_rms).then_inc(roots.sem, 1)

            def vector(self, dve):
                dve.wait_ge(roots.sem, self.root0 + 1)
                dve.reciprocal(rstd[:, :], rstd[:, :])
                dve.drain()
                for k in range(KD):
                    dve.scalar_tensor_tensor(xT[:, k, :], xT[:, k, :], col("g_final", k), rstd[:, :], ALU.mult, ALU.mult)

        class Attend(Stage):
            def __init__(self, q, k, v, pairs, k0=0, v0=0, keys=SEQ, masked=True, bias=None, shared=False, mix=False):
                super().__init__()
                self.q, self.k, self.v, self.pairs, self.k0, self.v0, self.keys = q, k, v, pairs, k0, v0, keys
                self.masked, self.bias, self.shared, self.mix = masked, bias, shared, mix
                self.dv = 2 * DH if mix else DH
                self.turn_lag = 3 if bias else 2
                self.value_lag = self.turn_lag + 1
                units = 8 * pairs
                self.staged0 = staged.reserve(pairs)
                self.logits0, self.turned0, self.value0 = logits_in.reserve(units), turned_in.reserve(units), value_in.reserve(units)
                self.max0, self.exp0, self.out0 = max_in.reserve(units), exp_in.reserve(units), head_out.reserve(units)
                self.tact0, self.tdve0 = turned_act.reserve(units // 2), turned_dve.reserve(units // 2)

            def unit(self, s):
                qt = s % 4
                return s // 8, s // 4 % 2, qt, (qt + 1) * P if self.masked else self.keys

            def turned_wait(self, eng, i, s):
                if s % 4 < 2:
                    eng.wait_ge(turned_act.sem, i * 8 + (self.tact0 + s // 4 * 2 + s % 4 + 1))
                    alone(eng, i)
                else:
                    eng.wait_ge(turned_dve.sem, i * 8 + (self.tdve0 + s // 4 * 2 + s % 4 - 1))
                    alone(eng, i)

            def tensor(self, pe):
                for i in turns(pe, self.pairs // 2):
                    for s in range(16 + self.value_lag):
                        if s < 16:
                            p, hh, qt, seen = self.unit(s)
                            if s % 8 == 0:
                                pe.wait_ge(staged.sem, i * 2 + (self.staged0 + p + 1))
                                alone(pe, i)
                            pe.wait_ge(exp_in.sem, i * 16 + (self.exp0 + s - 3))
                            alone(pe, i)
                            lo = hh * DH
                            keys = self.k[lo:lo + DH, self.k0, 0:seen] if self.shared else kS[lo:lo + DH, p, 0:seen]
                            mm = pe.matmul(ps[:, s % 4, 0:seen], qS[lo:lo + DH, p, qt * P:qt * P + P], keys,
                                           start=True, stop=True)
                            if self.masked and self.bias != "chosen":
                                mm = pe.matmul(ps[:, s % 4, seen - P:seen], identR[:, :], causalR[:, :], start=False, stop=True,
                                               skip_group_check=True)
                            mm.then_inc(logits_in.sem, 1)
                        t = s - self.turn_lag
                        if 0 <= t < 16:
                            p, hh, qt, seen = self.unit(t)
                            pe.wait_ge(exp_in.sem, i * 16 + (self.exp0 + t + 1))
                            alone(pe, i)
                            self.turned_wait(pe, i, t - 2)
                            for k in range(seen // P):
                                mm = pe.transpose(ps[:, 4 + t % 2, k * P:k * P + P], tmpA[:, t % 4, k * P:k * P + P], ident[:, :])
                            mm.then_inc(turned_in.sem, 1)
                        t = s - self.value_lag
                        if t >= 0:
                            p, hh, qt, seen = self.unit(t)
                            self.turned_wait(pe, i, t)
                            pe.wait_ge(head_out.sem, i * 16 + (self.out0 + t - 1))
                            alone(pe, i)
                            for k in range(seen // P):
                                values = self.value(i, p, k)
                                mm = pe.matmul(ps[:, 6 + t % 2, 0:2 * DH], tmpB[:, t % 2, k * P:k * P + P], values,
                                               start=(k == 0), stop=(k == seen // P - 1))
                            mm.then_inc(value_in.sem, 1)

            def value(self, i, p, k):
                if self.shared:
                    return self.v[:, k, 0:2 * DH]
                lo = i * (4 * DH) + p * 2 * DH
                return at(self.v, self.v0 + k, lo, lo + 2 * DH) if isinstance(lo, int) \
                    else self.v[:, self.v0 + k, bass.ds(lo, 2 * DH)]

            def stage(self, act, i, p):
                act.wait_ge(logits_in.sem, i * 16 + (self.logits0 + 8 * p - 8))
                alone(act, i)
                act.activation(qS[:, p, :], at(self.q, i * 2 + p), ACT.Copy, scale=SCALE)
                if not self.shared:
                    act.activation(kS[:, p, 0:self.keys], at(self.k, i * 2 + (p + self.k0), 0, self.keys), ACT.Copy)
                if self.bias == "gates":
                    for hh in range(2):
                        act.activation(gateS[:, 2 * p + hh, :], at(gate_rows, i * 4 + (2 * p + hh)), ACT.Copy)
                act.drain().then_inc(staged.sem, 1)

            def scalar(self, act):
                for i in turns(act, self.pairs // 2):
                    self.stage(act, i, 0)
                    self.stage(act, i, 1)
                    for s in range(16 + self.turn_lag):
                        if s < 16:
                            p, hh, qt, seen = self.unit(s)
                            act.wait_ge(max_in.sem, i * 16 + (self.max0 + s + 1))
                            alone(act, i)
                            act.wait_ge(turned_in.sem, i * 16 + (self.turned0 + s - 3))
                            alone(act, i)
                            src = tmpA[:, s % 4, 0:seen] if self.bias else ps[:, s % 4, 0:seen]
                            act.activation(tmpA[:, s % 4, 0:seen], src, ACT.Exp, bias=neg_max[:, s:s + 1],
                                           scale=-1.0 if self.bias else 1.0, accum_out=row_sum[:, s:s + 1]).then_inc(exp_in.sem, 1)
                        t = s - self.turn_lag
                        if t >= 0 and t % 4 < 2:
                            p, hh, qt, seen = self.unit(t)
                            act.wait_ge(turned_in.sem, i * 16 + (self.turned0 + t + 1))
                            alone(act, i)
                            act.wait_ge(value_in.sem, i * 16 + (self.value0 + t - 1))
                            alone(act, i)
                            act.activation(tmpB[:, t % 2, 0:seen], ps[:, 4 + t % 2, 0:seen], ACT.Copy).then_inc(turned_act.sem, 1)

            def vector(self, dve):
                for i in turns(dve, self.pairs // 2):
                    for s in range(16 + self.value_lag):
                        if s < 16:
                            p, hh, qt, seen = self.unit(s)
                            dve.wait_ge(logits_in.sem, i * 16 + (self.logits0 + s + 1))
                            alone(dve, i)
                            m = neg_max[:, s:s + 1]
                            if self.bias:
                                dve.wait_ge(turned_in.sem, i * 16 + (self.turned0 + s - 3))
                                alone(dve, i)
                                row = chosen[:, qt, 0:seen] if self.bias == "chosen" else gateS[:, 2 * p + hh, 0:seen]
                                dve.tensor_tensor_reduce(out=tmpA[:, s % 4, 0:seen], in0=ps[:, s % 4, 0:seen], in1=row, scale=-1.0,
                                                         scalar=-LOWEST, op0=ALU.add, op1=ALU.min, accum_out=m).then_inc(max_in.sem, 1)
                            else:
                                dve.tensor_reduce(m, ps[:, s % 4, 0:seen], AX.X, ALU.max, negate=True).then_inc(max_in.sem, 1)
                        t = s - self.turn_lag
                        if 0 <= t < 16 and t % 4 >= 2:
                            p, hh, qt, seen = self.unit(t)
                            dve.wait_ge(turned_in.sem, i * 16 + (self.turned0 + t + 1))
                            alone(dve, i)
                            dve.wait_ge(value_in.sem, i * 16 + (self.value0 + t - 1))
                            alone(dve, i)
                            dve.tensor_copy(tmpB[:, t % 2, 0:seen], ps[:, 4 + t % 2, 0:seen]).then_inc(turned_dve.sem, 1)
                        t = s - self.value_lag
                        if t >= 0:
                            p, hh, qt, seen = self.unit(t)
                            dve.wait_ge(value_in.sem, i * 16 + (self.value0 + t + 1))
                            alone(dve, i)
                            inv = row_inv[:, t:t + 1]
                            dve.reciprocal(inv, row_sum[:, t:t + 1])
                            dve.drain()
                            lo = qt * P + (0 if self.mix else hh * DH)
                            mine = 0 if self.mix or self.shared else hh * DH
                            to, o = at(self.q, i * 2 + p, lo, lo + self.dv), ps[:, 6 + t % 2, mine:mine + self.dv]
                            if self.mix and hh:
                                dve.tensor_scalar(inv, inv, neg_lam, None, ALU.mult)
                                dve.drain()
                                dve.scalar_tensor_tensor(to, o, inv, to, ALU.mult, ALU.add).then_inc(head_out.sem, 1)
                            else:
                                dve.tensor_scalar(to, o, inv, None, ALU.mult).then_inc(head_out.sem, 1)

        class QueryProducts(Products):
            def __init__(self, prepare, *made):
                super().__init__(prepare, *made)
                self.logged0 = gates.reserve(1)

            def scalar(self, act):
                self.prepare.scalar(act)
                act.wait_ge(lows.sem, self.prepare.low0 + KD)
                act.activation(tmpA[0:FOX, 0, :], gate[0:FOX, :], ACT.Abs)
                act.drain()
                act.activation(tmpA[0:FOX, 0, :], tmpA[0:FOX, 0, :], ACT.Exp, scale=-1.0)
                act.drain()
                act.activation(tmpA[0:FOX, 1, :], tmpA[0:FOX, 0, :], ACT.Ln, bias=1.0).then_inc(gates.sem, 1)
                for run in self.runs:
                    run.take.scalar(act)

            def vector(self, dve):
                self.prepare.vector(dve)
                for h in range(FOX):
                    dve.tensor_scalar(pick[:, h, :], ones[:, :], ident[:, h:h + 1], None, ALU.mult)
                dve.drain()
                dve.memset(tmpB[0:FOX, 0, :], 1.0)
                dve.wait_ge(gates.sem, self.logged0 + 1)
                dve.scalar_tensor_tensor(tmpB[0:FOX, 1, :], gate[0:FOX, :], 0.0, tmpA[0:FOX, 1, :], ALU.min, ALU.subtract)
                dve.drain()
                dve.tensor_tensor_scan(gate[0:FOX, :], tmpB[0:FOX, 0, :], tmpB[0:FOX, 1, :], 0.0, ALU.mult, ALU.add)
                for run in self.runs:
                    run.take.vector(dve)

        class GateRows(Stage):
            def __init__(self):
                super().__init__()
                self.turn0, self.high0 = turned_heads.reserve(FOX), highs.reserve(FOX)

            def tensor(self, pe):
                for h in range(FOX):
                    pe.wait_ge(highs.sem, self.high0 + h - 3)
                    pe.matmul(ps[:, h % 4, :], pick[0:FOX, h, :], gate[0:FOX, :], start=True, stop=True).then_inc(turned_heads.sem, 1)

            def scalar(self, act):
                for h in range(FOX):
                    act.wait_ge(turned_heads.sem, self.turn0 + h + 1)
                    act.activation(gate_rows[:, h, :], ps[:, h % 4, :], ACT.Copy, scale=-1.0).then_inc(highs.sem, 1)

        class Choose(Stage):
            ROUNDS = TOPK // 8
            def __init__(self):
                super().__init__()
                units = IDX * (QT - 1)
                self.index0, self.relu0, self.used0 = index_in.reserve(units), relus.reserve(units), scored.reserve(units)
                self.units = [(h, qt) for h in range(IDX) for qt in range(1, QT)]

            def tensor(self, pe):
                for n, (h, qt) in enumerate(self.units):
                    pe.wait_ge(relus.sem, self.relu0 + n - 3)
                    lo, seen = h % 2 * DH, (qt + 1) * P
                    pe.matmul(ps[:, n % 4, 0:seen], ixQ[lo:lo + DH, h // 2, qt * P:qt * P + P], spK[lo:lo + DH, 1, 0:seen],
                              start=True, stop=True).then_inc(index_in.sem, 1)

            def scalar(self, act):
                for n, (h, qt) in enumerate(self.units):
                    seen = (qt + 1) * P
                    act.wait_ge(index_in.sem, self.index0 + n + 1)
                    act.wait_ge(scored.sem, self.used0 + n - 3)
                    act.activation(tmpA[:, n % 4, 0:seen], ps[:, n % 4, 0:seen], ACT.Relu, scale=SCALE).then_inc(relus.sem, 1)

            def vector(self, dve):
                dve.tensor_copy(chosen[:, 0, 0:P], causal[:, :])
                dve.memset(spV[:, :, DH + IDX:P], 0.0)
                dve.tensor_scalar(spV[:, :, DH:DH + IDX], spV[:, :, DH:DH + IDX], IDX ** -0.5, None, ALU.mult)
                dve.drain()
                for n, (h, qt) in enumerate(self.units):
                    seen = (qt + 1) * P
                    dve.wait_ge(relus.sem, self.relu0 + n + 1)
                    weight, to = spV[:, qt, DH + h:DH + h + 1], chosen[:, qt, 0:seen]
                    if h == 0:
                        dve.tensor_scalar(to, tmpA[:, n % 4, 0:seen], weight, None, ALU.mult).then_inc(scored.sem, 1)
                    else:
                        dve.scalar_tensor_tensor(to, tmpA[:, n % 4, 0:seen], weight, to, ALU.mult, ALU.add).then_inc(scored.sem, 1)
                    dve.drain()
                for qt in range(1, QT):
                    mine = chosen[:, qt, qt * P:qt * P + P]
                    dve.tensor_tensor(mine, mine, causal[:, :], ALU.add)
                dve.drain()

            def round(self, dve):
                for qt in range(1, QT):
                    dve.max(top8[:, qt - 1, :], chosen[:, qt, 0:(qt + 1) * P])
                dve.drain()
                for qt in range(1, QT):
                    t = chosen[:, qt, 0:(qt + 1) * P]
                    dve.match_replace(t, top8[:, qt - 1, :], t, TAKEN)
                dve.drain()

            def finish(self, dve):
                for qt in range(1, QT):
                    t = chosen[:, qt, 0:(qt + 1) * P]
                    dve.tensor_scalar(t, t, LOWEST, MASKED, ALU.is_gt, ALU.mult)

        class Stick(Stage):
            FIRST = [0, 512, 896, 1152]
            PAIRS = 4

            def __init__(self, choose):
                super().__init__()
                self.choose = choose
                self.staged0, self.z0, self.log0, self.keep0 = staged.reserve(4), stick_z.reserve(32), stick_log.reserve(8), stick_keep.reserve(8)
                self.sum0, self.wt0, self.pv0, self.out0 = stick_sum.reserve(8), stick_wt.reserve(8), stick_pv.reserve(8), stick_out.reserve(8)

            def logits(self, pe, i, h):
                if h == 0:
                    pe.wait_ge(staged.sem, i + (self.staged0 + 1))
                    alone(pe, i)
                pe.wait_ge(stick_out.sem, i * 2 + (self.out0 + h - 1))
                alone(pe, i)
                lo = h * DH
                for k in range(QT):
                    n = SEQ - k * P
                    bank = ps[:, 4 * h + k, :]
                    pe.matmul(bank[:, 0:n], stickK[lo:lo + DH, k * P:k * P + P], stickQ[lo:lo + DH, k * P:SEQ], start=True, stop=True)
                    pe.matmul(bank[:, 0:P], identR[:, :], beforeR[:, :], start=False, stop=True, skip_group_check=True
                              ).then_inc(stick_z.sem, 1)

            def sums(self, pe, i, h):
                pe.wait_ge(stick_keep.sem, i * 2 + (self.keep0 + h + 1))
                alone(pe, i)
                hh = h % 2
                for k in range(QT):
                    n = SEQ - k * P
                    for k2 in range(k, QT):
                        m = SEQ - k2 * P
                        mm = pe.matmul(ps[:, 4 * hh + k, n - m:n], (neg_tri if k2 == k else neg_ones)[:, :],
                                       keep[:, hh, self.FIRST[k2]:self.FIRST[k2] + m], start=False, stop=True, skip_group_check=True)
                mm.then_inc(stick_sum.sem, 1)

            def values(self, pe, i, h):
                pe.wait_ge(stick_wt.sem, i * 2 + (self.wt0 + h + 1))
                alone(pe, i)
                hh = h % 2
                lo = i * (2 * DH) + h // 2 * (2 * DH)
                for qt in range(QT):
                    bank, to = (4 * hh + 3, P + qt * P) if qt < 3 else (4 * hh + 2, 2 * P)
                    for k in range(qt + 1):
                        w0 = self.FIRST[k] + (qt - k) * P
                        v = stV[:, k, lo:lo + 2 * DH] if isinstance(lo, int) else stV[:, k, bass.ds(lo, 2 * DH)]
                        pe.matmul(ps[:, bank, to:to + P], stick_w[:, hh, w0:w0 + P], v,
                                  start=(k == 0), stop=(k == qt))
                pe.drain().then_inc(stick_pv.sem, 1)

            def tensor(self, pe):
                self.logits(pe, 0, 0)
                self.sums(pe, 0, 0)
                self.logits(pe, 0, 1)
                self.values(pe, 0, 0)
                for i in turns(pe, self.PAIRS, 1):
                    self.logits(pe, i, 0)
                    self.sums(pe, i, -1)
                    self.sums(pe, i, 0)
                    self.values(pe, i, -1)
                    self.logits(pe, i, 1)
                    self.values(pe, i, 0)
                self.sums(pe, self.PAIRS, -1)
                self.values(pe, self.PAIRS, -1)

            def stage(self, act, i):
                act.wait_ge(stick_z.sem, i * 8 + self.z0)
                alone(act, i)
                act.activation(stickQ[:, :], at(stQ, i), ACT.Copy, scale=SCALE)
                act.activation(stickK[:, :], at(stK, i), ACT.Copy)
                act.drain().then_inc(staged.sem, 1)

            def logs(self, act, i, h):
                act.wait_ge(stick_pv.sem, i * 2 + (self.pv0 + h - 1))
                alone(act, i)
                e = stick_w[:, h, :]
                for k in range(QT):
                    n = SEQ - k * P
                    act.wait_ge(stick_z.sem, i * 8 + (self.z0 + 4 * h + k + 1))
                    alone(act, i)
                    act.activation(e[:, self.FIRST[k]:self.FIRST[k] + n], ps[:, 4 * h + k, 0:n], ACT.Abs)
                act.drain()
                act.activation(e, e, ACT.Exp, scale=-1.0)
                act.drain()
                act.activation(e, e, ACT.Ln, bias=1.0).then_inc(stick_log.sem, 1)

            def weights(self, act, i, h):
                act.wait_ge(stick_sum.sem, i * 2 + (self.sum0 + h + 1))
                alone(act, i)
                hh = h % 2
                for k in range(QT):
                    n = SEQ - k * P
                    last = act.activation(stick_w[:, hh, self.FIRST[k]:self.FIRST[k] + n], ps[:, 4 * hh + k, 0:n], ACT.Exp)
                last.then_inc(stick_wt.sem, 1)

            def scalar(self, act):
                self.stage(act, 0)
                self.logs(act, 0, 0)
                self.weights(act, 0, 0)
                self.stage(act, 1)
                self.logs(act, 0, 1)
                for i in turns(act, self.PAIRS - 1, 1):
                    self.logs(act, i, 0)
                    self.weights(act, i, -1)
                    self.weights(act, i, 0)
                    self.stage(act, i + 1)
                    self.logs(act, i, 1)
                last = self.PAIRS - 1
                self.logs(act, last, 0)
                self.weights(act, last, -1)
                self.weights(act, last, 0)
                self.logs(act, last, 1)
                self.weights(act, last, 1)

            def keeps(self, dve, i, h):
                dve.wait_ge(stick_log.sem, i * 2 + (self.log0 + h + 1))
                alone(dve, i)
                for k in range(QT):
                    n = SEQ - k * P
                    f = self.FIRST[k]
                    last = dve.scalar_tensor_tensor(keep[:, h, f:f + n], ps[:, 4 * h + k, 0:n], 0.0, stick_w[:, h, f:f + n],
                                                    ALU.max, ALU.add)
                last.then_inc(stick_keep.sem, 1)

            def outputs(self, dve, i, h):
                dve.wait_ge(stick_pv.sem, i * 2 + (self.pv0 + h + 1))
                alone(dve, i)
                hh = h % 2
                to = at(stQ, i + h // 2).rearrange("p (t c) -> p t c", t=QT)[:, :, hh * DH:hh * DH + DH]
                mine = ps[:, 4 * hh + 3, P:SEQ].rearrange("p (t c) -> p t c", t=3)[:, :, hh * DH:hh * DH + DH]
                dve.tensor_copy(to[:, 0:3, :], mine)
                dve.tensor_copy(to[:, 3, :], ps[:, 4 * hh + 2, 2 * P + hh * DH:2 * P + hh * DH + DH])
                dve.drain().then_inc(stick_out.sem, 1)

            def vector(self, dve):
                self.keeps(dve, 0, 0)
                self.choose.round(dve)
                self.outputs(dve, 0, 0)
                self.keeps(dve, 0, 1)
                for i in turns(dve, self.PAIRS, 1):
                    self.keeps(dve, i, 0)
                    self.choose.round(dve)
                    self.outputs(dve, i, -1)
                    self.choose.round(dve)
                    self.outputs(dve, i, 0)
                    self.choose.round(dve)
                    self.keeps(dve, i, 1)
                    self.choose.round(dve)
                for i in turns(dve, Choose.ROUNDS - 1 - 4 * (self.PAIRS - 1)):
                    self.choose.round(dve)
                self.outputs(dve, self.PAIRS, -1)
                self.choose.finish(dve)

        class SubNorm(Stage):
            def __init__(self):
                super().__init__()
                self.square0, self.root0 = squares.reserve(8), roots.reserve(1)
                self.low0 = lows.reserve(8)

            def scalar(self, act):
                for h in range(8):
                    act.wait_ge(lows.sem, self.low0 + h - 3)
                    act.activation(tmpA[:, h % 4, :], difQ[:, h, :], ACT.Square).then_inc(squares.sem, 1)
                act.wait_ge(lows.sem, self.low0 + 8)
                act.activation(head_std, head_sq, ACT.Sqrt, bias=eps_ln, scale=1.0 / P).then_inc(roots.sem, 1)

            def vector(self, dve):
                for h in range(8):
                    dve.wait_ge(squares.sem, self.square0 + h + 1)
                    dve.tensor_reduce(head_sq[:, 4 * h:4 * h + 4], tmpA[:, h % 4, :].rearrange("p (t c) -> p t c", t=QT), AX.X, ALU.add
                                      ).then_inc(lows.sem, 1)
                dve.wait_ge(roots.sem, self.root0 + 1)
                dve.reciprocal(head_sq, head_std)
                dve.drain()
                for n in range(32):
                    t = difQ[:, n // 4, n % 4 * P:n % 4 * P + P]
                    dve.tensor_scalar(t, t, head_sq[:, n:n + 1], None, ALU.mult)
                g = cols[:, row_of["subln"]:row_of["subln"] + 1]
                dve.tensor_scalar(g, g, 1.0 - LAMBDA_INIT, None, ALU.mult)

        class Output(Stage):
            def __init__(self):
                super().__init__()
                self.turn0, self.high0 = turned_heads.reserve(KD), highs.reserve(KD)

            def tensor(self, pe):
                for n in range(KD):
                    pe.wait_ge(highs.sem, self.high0 + n - 3)
                    t, h = n // 2, n % 2
                    for k in range(4):
                        last = pe.transpose(ps[:, n % 4, k * P:k * P + P], xT[:, 4 * h + k, t * P:t * P + P], ident[:, :])
                    last.then_inc(turned_heads.sem, 1)

            def scalar(self, act):
                for n in range(KD):
                    act.wait_ge(turned_heads.sem, self.turn0 + n + 1)
                    act.activation(tok_out[:, n // 2, n % 2 * 512:n % 2 * 512 + 512], ps[:, n % 4, :], ACT.Copy).then_inc(highs.sem, 1)

        Constants()
        Tables()
        mem_w = a["w_mem_kv"]
        Products(RmsParts(memT, "g_mem", n=MEM),
                 *[Run("A", 1, KD, plain(mem_w[l]), TakeCopy(memK, MEM, 2 * l), tokens=MEM) if kind == "k" else
                   Run("B", 1, KD, plain(mem_w[l], MEM), TakeMemV(l), tokens=MEM) for l in range(2) for kind in "kv"])
        Lambda()
        w = a["w_in_a"][0]
        Products(RmsParts(xT, "g_mix", 0),
                 Run("A", NCONV, KD, pairs_of(w, 0, w, CONV), TakeGlu()),
                 Run("A", 1, KD, plain(w, 2 * CONV), TakeCopy(q_mem0)))
        modulation = Modulation()
        Attend(q_mem0, memK, memV, 2, k0=0, v0=0, keys=MEM, masked=False)
        Conv(modulation)
        ModTurn()
        ModBias()
        LayerNorm(y, NCONV, "ln_g", "ln_b", silu=True, summed_up=False)
        Products(HeadParts([(q_mem0, 0), (q_mem0, 1)], first=NCONV), Run("A", 4, KD, plain(a["w_out"][0]), TakeResidual(then="square")))

        def conv_ff(l):
            FeedForward(RmsParts(xT, "g_ffn", KD * l, stats="acc"), lambda h: pairs_of(a["w_up"][l], h * HALF * P, a["w_up"][l], FF + h * HALF * P),
                        a["w_down"][l], "square", conv=l)
        conv_ff(0)
        w = a["w_kvf"]
        Products(RmsParts(xT, "g_kv", stats="acc"),
                 Run("A", 3, KD, plain(w), TakeCopy(foxK)),
                 Run("B", 3, KD, plain(w, CONV), TakeValues(foxV)),
                 Run("A", 1, KD, lambda s: [(0, FOX, columns(w, 2 * CONV, FOX)), (FOX, P, columns(w, 0, P - FOX))],
                     TakeForget(), width=P))
        w_b = a["w_in_b"][0]
        QueryProducts(RmsParts(xT, "g_mix", KD, stats="none"),
                      Run("A", 3, KD, plain(w_b), TakeCopy(foxQ)),
                      Run("A", 1, KD, plain(w_b, CONV), TakeCopy(q_mem1)))
        GateRows()
        Attend(foxQ, foxK, foxV, 6, bias="gates")
        Attend(q_mem1, memK, memV, 2, k0=2, v0=2, keys=MEM, masked=False)
        Products(HeadParts([(foxQ, t) for t in range(6)] + [(q_mem1, 0), (q_mem1, 1)]),
                 Run("A", 4, KD, plain(a["w_out"][1]), TakeResidual(then="square")))
        conv_ff(1)
        FinalRms()

        def gain(l, chunk):
            return 48 * l + KD * chunk

        def gated_ff(l):
            FeedForward(ModParts(l, 3, 4), lambda h: pairs_of(a["w_gate_2"][l], h * HALF * P, a["w_up_2"][l], h * HALF * P),
                        a["w_down_2"][l], "sum", gain=gain(l, 5))
            LayerNorm(xT, KD, "ln_ffn_g", "ln_ffn_b", KD * l)
        w_e = a["w_in_even_2"][0]
        Products(ModParts(0, 0, 1),
                 Run("A", 2, KD, plain(w_e, 0), TakeCopy(stQ)),
                 Run("A", 2, KD, plain(w_e, 512), TakeCopy(stK)),
                 Run("B", 2, KD, plain(w_e, 1024), TakeValues(stV)),
                 Run("A", 2, KD, plain(w_e, 1536), TakeRope(spQ)),
                 Run("A", 1, KD, lambda s: [(0, 64, columns(w_e, 2048, 64)), (64, 128, columns(w_e, 2048, 64)),
                                            (128, 192, columns(w_e, 2432, 64)), (192, 256, columns(w_e, 2432, 64))],
                     TakeRope(spK)),
                 Run("A", 1, KD, plain(w_e, 2176), TakeRope(ixQ)),
                 Run("B", 1, KD, lambda s: [(0, 64, columns(w_e, 2112, 64)), (64, 68, columns(w_e, 2496, 4))],
                     TakeValues(spV), width=68))
        choose = Choose()
        Stick(choose)
        Attend(spQ, spK, spV, 4, bias="chosen", shared=True)
        Products(HeadParts([(stQ, t) for t in range(4)] + [(spQ, t) for t in range(4)]),
                 Run("A", 4, KD, plain(a["w_out_even_2"][0]), TakeResidual(gain(0, 2), "sum")))
        LayerNorm(xT, KD, "ln_mix_g", "ln_mix_b", 0)
        gated_ff(0)
        w_o = a["w_in_odd_2"][0]
        Products(ModParts(1, 0, 1),
                 Run("A", 4, KD, plain(w_o, 0), TakeRope(difQ)),
                 Run("A", 4, KD, plain(w_o, D), TakeRope(difK)),
                 Run("B", 4, KD, plain(w_o, 2 * D), TakeValues(difV)))
        Attend(difQ, difK, difV, 8, mix=True)
        SubNorm()
        Products(HeadParts([(difQ, t) for t in range(8)], gain=col("subln", 0)),
                 Run("A", 4, KD, plain(a["w_out_odd_2"][0]), TakeResidual(gain(1, 2), "sum")))
        LayerNorm(xT, KD, "ln_mix_g", "ln_mix_b", KD)
        gated_ff(1)
        output = Output()

        vector_loads = []
        for name, v in vectors:
            r0, n = row_of[name], v.shape[0]
            while n:
                m = min(n, P - r0 % P)
                k = r0 - row_of[name]
                vector_loads.append((vec_rows[r0 % P:r0 % P + m, r0 // P, :], v[k:k + m, :]))
                r0, n = r0 + m, n - m

        for name in ("pe", "act", "dve", "pool", "sp"):
            turn[name] = sem(name + "_turn")
        block = ctx.enter_context(nc.Block())

        @block.sync
        def _(sp):
            turn[id(sp)] = turn["sp"]
            sp.dma_start(tok_mem[:, :, :], a["mem"][0].rearrange("(t p) d -> p t d", p=P)).then_inc(tokens_in, 16)
            sp.dma_start(tok_x[:, :, :], a["x"][0].rearrange("(t p) d -> p t d", p=P)).then_inc(tokens_in, 16)
            sp.dma_start(rope_const, a["rope_const"]).then_inc(tables_in, 16)
            sp.dma_start(gate_bias[0:FOX, :], a["b_f"].rearrange("(h o) -> h o", o=1)).then_inc(tables_in, 16)
            sp.dma_start(pos_int[:, :], a["positions_2"][0].partition_broadcast(P)).then_inc(tables_in, 16)
            for n, name in enumerate(("lam_q1_2", "lam_k1_2", "lam_q2_2", "lam_k2_2")):
                sp.dma_start(lams[:, n, :], a[name][0].partition_broadcast(P)).then_inc(tables_in, 16)
            sp.wait_ge(constants_in, 1)
            for to, src in vector_loads[0::2]:
                sp.dma_start(to, src).then_inc(vectors_in, 16)
            for run in runs:
                run.load(sp)
            for t in range(QT):
                sp.wait_ge(highs.sem, output.high0 + 2 * t + 2)
                sp.dma_start(out[0][t * P:t * P + P, :], tok_out[:, t, :]).then_inc(out_written, 16)
            sp.wait_ge(out_written, 16 * QT)

        @block.gpsimd
        def _(pool):
            turn[id(pool)] = turn["pool"]
            start_signals(pool, "pool")
            pool.sem_inc(raw_free[0], 1)
            pool.sem_inc(raw_free[1], 1)
            for free in mod_free:
                pool.sem_inc(free, 1)
            pool.memset(ident[:, :], 0.0)
            pool.memset(ones[:, :], 1.0)
            pool.memset(mean_of[:, :], 1.0 / D)
            pool.memset(causal[:, :], 0.0)
            pool.memset(before[:, :], 0.0)
            pool.memset(neg_tri[:, :], -1.0)
            pool.memset(neg_ones[:, :], -1.0)
            pool.memset(silu_c[:, :, :], 0.0)
            pool.memset(vec_rows[:, VT - 1, :], 0.0)
            pool.drain()
            pool.affine_select(out=ident[:, :], in_=ident[:, :], compare_op=ALU.not_equal, fill=1.0, base=0,
                               pattern=[[-1, P]], channel_multiplier=1)
            pool.affine_select(out=causal[:, :], in_=causal[:, :], compare_op=ALU.is_ge, fill=MASKED, base=0,
                               pattern=[[-1, P]], channel_multiplier=1)
            pool.affine_select(out=before[:, :], in_=before[:, :], compare_op=ALU.is_ge, fill=MASKED, base=-1,
                               pattern=[[1, P]], channel_multiplier=-1)
            pool.affine_select(out=neg_tri[:, :], in_=neg_tri[:, :], compare_op=ALU.is_ge, fill=0.0, base=0,
                               pattern=[[-1, P]], channel_multiplier=1)
            pool.drain().then_inc(constants_in, 1)
            for run in runs:
                run.split(pool)

        @block.tensor
        def _(pe):
            turn[id(pe)] = turn["pe"]
            start_signals(pe, "pe")
            for n, stage in enumerate(stages):
                if n:
                    pe.wait_ge(scalar_done, n)
                    pe.wait_ge(vector_done, n)
                stage.tensor(pe)
                pe.drain().then_inc(tensor_done, 1)

        @block.scalar
        def _(act):
            turn[id(act)] = turn["act"]
            start_signals(act, "act")
            act.wait_ge(constants_in, 1)
            for to, src in vector_loads[1::2]:
                act.dma_start(to, src).then_inc(vectors_in, 16)
            for n, stage in enumerate(stages):
                if n:
                    act.wait_ge(tensor_done, n)
                    act.wait_ge(vector_done, n)
                stage.scalar(act)
                act.drain().then_inc(scalar_done, 1)

        @block.vector
        def _(dve):
            turn[id(dve)] = turn["dve"]
            start_signals(dve, "dve")
            for n, stage in enumerate(stages):
                if n:
                    dve.wait_ge(tensor_done, n)
                    dve.wait_ge(scalar_done, n)
                stage.vector(dve)
                dve.drain().then_inc(vector_done, 1)


_INS = ["x", "mem", "g_mix", "w_in_a", "b_glu", "w_dw_a", "b_dw_a", "ln_g", "ln_b", "g_kv", "w_kvf", "b_f", "w_in_b", "g_mem",
        "w_mem_kv", "w_out", "g_ffn", "w_up", "w_dw_f", "b_dw_f", "w_down", "g_final", "c_2", "positions_2", "w_mod_2",
        "b_mod_2", "w_in_even_2", "w_out_even_2", "w_in_odd_2", "lam_q1_2", "lam_k1_2", "lam_q2_2", "lam_k2_2",
        "subln_g_2", "w_out_odd_2", "ln_mix_g_2", "ln_mix_b_2", "w_gate_2", "w_up_2", "w_down_2", "ln_ffn_g_2", "ln_ffn_b_2"]


def kernel(**inputs):
    import numpy as np
    import concourse.bacc as bacc
    from concourse.bass_utils import run_bass_kernel_spmd

    nc = bacc.Bacc("TRN2", target_bir_lowering=False, num_devices=1)
    arrays = {name: np.ascontiguousarray(inputs[name]) for name in _INS}
    inverse = np.float32(10000.0) ** (-np.arange(0, DH, 2, dtype=np.float32) / np.float32(DH))
    lane = np.arange(P)
    arrays["rope_const"] = np.stack([inverse[lane % (DH // 2)], np.where(lane % DH < DH // 2, -1.0, 1.0)], axis=1).astype(np.float32)
    aps = {name: nc.dram_tensor(name, v.shape, mybir.dt.from_np(v.dtype), kind="ExternalInput").ap() for name, v in arrays.items()}
    out = nc.dram_tensor("out", (1, SEQ, D), F32, kind="ExternalOutput").ap()
    build(nc, aps, out)
    return run_bass_kernel_spmd(nc, [arrays], core_ids=[0]).results[0]["out"]
```
